# Optimizing a Trainium2 kernel written in Bass

```python
import math
import jax, jax.numpy as jnp
from jax import lax
import numpy as np

D_MODEL = 1024
BATCH = 1
SEQ = 1024
DEPTH = 1

GRID_W = 64
CTX_LEN = 256
D_S5 = 512
S5_GROUP = 16
S5_GROUPS = D_S5 // S5_GROUP
S5_STATE = 64
DT_MIN = 0.001
DT_MAX = 0.1
D_LRU = D_MODEL - D_S5
LRU_HEADS = 8
LRU_HEAD_DIM = D_LRU // LRU_HEADS
LRU_CONV = 4
CONV_LEFT = 2
LRU_C = 8.0
D_IN = D_S5 + 2 * D_LRU
N_GROUPS = 4
EXPERTS_PER_GROUP = 4
N_EXPERTS = N_GROUPS * EXPERTS_PER_GROUP
TOP_K = 2
D_EXPERT = 512
EPS = 1e-6
F32 = jnp.float32

kernel_name = 'hybrid_s5_rglru_hmoe_prefix_dit'

def rmsnorm(x, g):
    xf = x.astype(F32)
    y = xf * lax.rsqrt(jnp.mean(xf * xf, axis=-1, keepdims=True) + EPS)
    return (y * g.astype(F32)).astype(x.dtype)

def modulate(x, shift, scale):
    return x * (1 + scale) + shift

def to_cols(x, rows):
    b, l, ch = x.shape
    return x.reshape(b, rows, GRID_W, ch).transpose(0, 2, 1, 3).reshape(b, l, ch)

def from_cols(x, rows):
    b, l, ch = x.shape
    return x.reshape(b, GRID_W, rows, ch).transpose(0, 2, 1, 3).reshape(b, l, ch)

def linear_scan(a, b, h0, reverse):
    def combine(left, right):
        a_l, b_l = left
        a_r, b_r = right
        return a_r * a_l, a_r * b_l + b_r
    a_cum, h = lax.associative_scan(combine, (a, b), axis=1, reverse=reverse)
    if h0 is not None:
        h = h + a_cum * h0[:, None]
    return h

def s5_discretize(a_re, a_im, log_dt, b_re, b_im):
    lam = lax.complex(a_re.astype(F32), a_im.astype(F32))
    dt = jnp.exp(log_dt.astype(F32))[:, None]
    a_bar = jnp.exp(lam * dt)
    b = lax.complex(b_re.astype(F32), b_im.astype(F32))
    b_bar = ((a_bar - 1) / lam)[..., None] * b
    return a_bar, b_bar

def s5_states(u, h0, a_bar, b_bar, reverse):
    bu = jnp.einsum('blgh,gph->blgp', u.astype(jnp.complex64), b_bar)
    a = jnp.broadcast_to(a_bar, (1, u.shape[1]) + a_bar.shape)
    return linear_scan(a, bu, h0, reverse)

def s5_readout(y, u, d_skip, w_glu, b_glu, dtype):
    b, l = u.shape[:2]
    y = (y + d_skip.astype(F32).reshape(S5_GROUPS, S5_GROUP) * u).reshape(b, l, D_S5)
    z = jax.nn.gelu(y)
    return (z * jax.nn.sigmoid(z @ w_glu.astype(F32) + b_glu.astype(F32))).astype(dtype)

def s5_mixer(u_ctx, u_lat, a_re, a_im, log_dt, b_re, b_im, c_re, c_im, d_skip, w_glu, b_glu,
             need_ctx, dtype):
    uc = u_ctx.astype(F32).reshape(u_ctx.shape[:2] + (S5_GROUPS, S5_GROUP))
    ul = u_lat.astype(F32).reshape(u_lat.shape[:2] + (S5_GROUPS, S5_GROUP))
    y_lat = 0.0
    y_ctx = 0.0
    for d, reverse in enumerate((False, True)):
        a_bar, b_bar = s5_discretize(a_re[d], a_im[d], log_dt[d], b_re[d], b_im[d])
        cmat = lax.complex(c_re[d].astype(F32), c_im[d].astype(F32))
        h_ctx = s5_states(uc, None, a_bar, b_bar, reverse)
        h0 = h_ctx[:, 0] if reverse else h_ctx[:, -1]
        h_lat = s5_states(ul, h0, a_bar, b_bar, reverse)
        y_lat = y_lat + jnp.einsum('blgp,ghp->blgh', h_lat, cmat).real
        if need_ctx:
            y_ctx = y_ctx + jnp.einsum('blgp,ghp->blgh', h_ctx, cmat).real
    out_lat = s5_readout(y_lat, ul, d_skip, w_glu, b_glu, dtype)
    out_ctx = s5_readout(y_ctx, uc, d_skip, w_glu, b_glu, dtype) if need_ctx else None
    return out_lat, out_ctx

def dwconv_centred(x, w, b):
    l = x.shape[1]
    xp = jnp.pad(x, ((0, 0), (CONV_LEFT, LRU_CONV - 1 - CONV_LEFT), (0, 0)))
    y = b
    for k in range(LRU_CONV):
        y = y + w[k] * xp[:, k:k + l]
    return y

def rglru_coeffs(xc, w_a, b_a, w_x, b_x, lam):
    bsz, l, _ = xc.shape
    xh = xc.reshape(bsz, l, LRU_HEADS, LRU_HEAD_DIM)
    r = jax.nn.sigmoid(jnp.einsum('blhi,hij->blhj', xh, w_a.astype(F32)).reshape(bsz, l, D_LRU)
                       + b_a.astype(F32))
    i = jax.nn.sigmoid(jnp.einsum('blhi,hij->blhj', xh, w_x.astype(F32)).reshape(bsz, l, D_LRU)
                       + b_x.astype(F32))
    log_a = -LRU_C * r * jax.nn.softplus(-lam.astype(F32))
    a = jnp.exp(log_a)
    b = jnp.sqrt(-jnp.expm1(2 * log_a)) * (i * xc)
    return a, b

def rglru_mixer(x_ctx, g_ctx, x_lat, g_lat, rows, conv_w, conv_b, w_a, b_a, w_x, b_x, lam,
                need_ctx, dtype):
    cw = conv_w.astype(F32)
    cb = conv_b.astype(F32)
    xc_ctx = dwconv_centred(x_ctx.astype(F32), cw, cb)
    xc_lat = dwconv_centred(to_cols(x_lat.astype(F32), rows), cw, cb)
    h_lat = 0.0
    h_ctx = 0.0
    for d, reverse in enumerate((False, True)):
        a, b = rglru_coeffs(xc_ctx, w_a[d], b_a[d], w_x[d], b_x[d], lam[d])
        hc = linear_scan(a, b, None, reverse)
        h0 = hc[:, 0] if reverse else hc[:, -1]
        a, b = rglru_coeffs(xc_lat, w_a[d], b_a[d], w_x[d], b_x[d], lam[d])
        h_lat = h_lat + linear_scan(a, b, h0, reverse)
        if need_ctx:
            h_ctx = h_ctx + hc
    out_lat = (from_cols(h_lat, rows) * jax.nn.gelu(g_lat.astype(F32))).astype(dtype)
    out_ctx = (h_ctx * jax.nn.gelu(g_ctx.astype(F32))).astype(dtype) if need_ctx else None
    return out_lat, out_ctx

def hier_moe(h, w_group, b_group, w_router, b_router, w1, w3, w2):
    shp = h.shape
    t = h.reshape(-1, shp[-1])
    tf = t.astype(F32)
    group_prob = jax.nn.softmax(tf @ w_group.astype(F32) + b_group.astype(F32), axis=-1)
    g_p, g_idx = lax.top_k(group_prob, 1)
    exp_logits = jnp.einsum('td,gde->tge', tf, w_router.astype(F32)) + b_router.astype(F32)
    sel = jnp.einsum('tge,tg->te', exp_logits, jax.nn.one_hot(g_idx[:, 0], N_GROUPS, dtype=F32))
    e_p, e_idx = lax.top_k(jax.nn.softmax(sel, axis=-1), TOP_K)
    weights = g_p * e_p / jnp.sum(e_p, axis=-1, keepdims=True)
    expert_id = g_idx * EXPERTS_PER_GROUP + e_idx
    gates = jnp.einsum('tk,tke->te', weights,
                       jax.nn.one_hot(expert_id, N_EXPERTS, dtype=F32)).astype(h.dtype)
    out = jnp.zeros_like(t)
    for e in range(N_EXPERTS):
        hid = jax.nn.silu(t @ w1[e]) * (t @ w3[e])
        out = out + gates[:, e:e + 1] * (hid @ w2[e])
    return out.reshape(shp)

def setup_inputs(seed: int = 0) -> dict:
    key = jax.random.key(seed)
    ks = iter(jax.random.split(key, 48))

    def nrm(shape, std):
        return std * jax.random.normal(next(ks), shape, F32)

    L, D = DEPTH, D_MODEL
    G, P, H = S5_GROUPS, S5_STATE, S5_GROUP
    x = nrm((BATCH, SEQ, D), 1.0)
    c = nrm((BATCH, D), 1.0)
    ctx = nrm((BATCH, CTX_LEN, D), 1.0)
    c_ctx = nrm((D,), 1.0)
    w_mod = nrm((L, D, 6 * D), 0.5 * D ** -0.5)
    b_mod = nrm((L, 6 * D), 0.02)
    norm1_g = 1.0 + nrm((L, D), 0.02)
    norm2_g = 1.0 + nrm((L, D), 0.02)
    w_in = nrm((L, D, D_IN), D ** -0.5)
    w_out = nrm((L, D, D), D ** -0.5)
    n = jnp.arange(P, dtype=F32)
    s5_a_re = -0.5 + nrm((L, 2, G, P), 0.02)
    s5_a_im = math.pi * n + nrm((L, 2, G, P), 0.02)
    s5_log_dt = jax.random.uniform(next(ks), (L, 2, G), F32, math.log(DT_MIN), math.log(DT_MAX))
    s5_b_re = nrm((L, 2, G, P, H), (2 * H) ** -0.5)
    s5_b_im = nrm((L, 2, G, P, H), (2 * H) ** -0.5)
    s5_c_re = nrm((L, 2, G, H, P), P ** -0.5)
    s5_c_im = nrm((L, 2, G, H, P), P ** -0.5)
    s5_d = nrm((L, D_S5), 1.0)
    s5_w_glu = nrm((L, D_S5, D_S5), D_S5 ** -0.5)
    s5_b_glu = nrm((L, D_S5), 0.02)
    lru_conv_w = nrm((L, LRU_CONV, D_LRU), LRU_CONV ** -0.5)
    lru_conv_b = nrm((L, D_LRU), 0.02)
    lru_w_a = nrm((L, 2, LRU_HEADS, LRU_HEAD_DIM, LRU_HEAD_DIM), LRU_HEAD_DIM ** -0.5)
    lru_b_a = nrm((L, 2, D_LRU), 0.02)
    lru_w_x = nrm((L, 2, LRU_HEADS, LRU_HEAD_DIM, LRU_HEAD_DIM), LRU_HEAD_DIM ** -0.5)
    lru_b_x = nrm((L, 2, D_LRU), 0.02)
    a_c = jax.random.uniform(next(ks), (L, 2, D_LRU), F32, 0.9, 0.999)
    s = a_c ** (1.0 / LRU_C)
    lru_lam = jnp.log(s) - jnp.log1p(-s)
    moe_w_group = nrm((L, D, N_GROUPS), D ** -0.5)
    moe_b_group = nrm((L, N_GROUPS), 0.01)
    moe_w_router = nrm((L, N_GROUPS, D, EXPERTS_PER_GROUP), D ** -0.5)
    moe_b_router = nrm((L, N_GROUPS, EXPERTS_PER_GROUP), 0.01)
    moe_w1 = nrm((L, N_EXPERTS, D, D_EXPERT), D ** -0.5)
    moe_w3 = nrm((L, N_EXPERTS, D, D_EXPERT), D ** -0.5)
    moe_w2 = nrm((L, N_EXPERTS, D_EXPERT, D), D_EXPERT ** -0.5)
    final_g = 1.0 + nrm((D,), 0.02)
    return {'x': x, 'c': c, 'ctx': ctx, 'c_ctx': c_ctx, 'w_mod': w_mod, 'b_mod': b_mod,
            'norm1_g': norm1_g, 'norm2_g': norm2_g, 'w_in': w_in, 'w_out': w_out,
            's5_a_re': s5_a_re, 's5_a_im': s5_a_im, 's5_log_dt': s5_log_dt,
            's5_b_re': s5_b_re, 's5_b_im': s5_b_im, 's5_c_re': s5_c_re, 's5_c_im': s5_c_im,
            's5_d': s5_d, 's5_w_glu': s5_w_glu, 's5_b_glu': s5_b_glu,
            'lru_conv_w': lru_conv_w, 'lru_conv_b': lru_conv_b, 'lru_w_a': lru_w_a,
            'lru_b_a': lru_b_a, 'lru_w_x': lru_w_x, 'lru_b_x': lru_b_x, 'lru_lam': lru_lam,
            'moe_w_group': moe_w_group, 'moe_b_group': moe_b_group,
            'moe_w_router': moe_w_router, 'moe_b_router': moe_b_router,
            'moe_w1': moe_w1, 'moe_w3': moe_w3, 'moe_w2': moe_w2, 'final_g': final_g}

def reference(x, c, ctx, c_ctx, w_mod, b_mod, norm1_g, norm2_g, w_in, w_out,
              s5_a_re, s5_a_im, s5_log_dt, s5_b_re, s5_b_im, s5_c_re, s5_c_im,
              s5_d, s5_w_glu, s5_b_glu,
              lru_conv_w, lru_conv_b, lru_w_a, lru_b_a, lru_w_x, lru_b_x, lru_lam,
              moe_w_group, moe_b_group, moe_w_router, moe_b_router,
              moe_w1, moe_w3, moe_w2, final_g):
    rows = x.shape[1] // GRID_W
    dtype = x.dtype
    silu_c = jax.nn.silu(c)
    silu_cc = jax.nn.silu(c_ctx)
    xc = ctx
    n_ctx = ctx.shape[1]
    for l in range(DEPTH):
        need_ctx = l < DEPTH - 1
        mod = (silu_c @ w_mod[l] + b_mod[l])[:, None, :]
        modc = (silu_cc @ w_mod[l] + b_mod[l])[None, None, :]
        sh1, sc1, ga1, sh2, sc2, ga2 = jnp.split(mod, 6, axis=-1)
        sh1c, sc1c, ga1c, sh2c, sc2c, ga2c = jnp.split(modc, 6, axis=-1)

        p_lat = modulate(rmsnorm(x, norm1_g[l]), sh1, sc1) @ w_in[l]
        p_ctx = modulate(rmsnorm(xc, norm1_g[l]), sh1c, sc1c) @ w_in[l]
        u_lat, r_lat, q_lat = jnp.split(p_lat, [D_S5, D_S5 + D_LRU], axis=-1)
        u_ctx, r_ctx, q_ctx = jnp.split(p_ctx, [D_S5, D_S5 + D_LRU], axis=-1)
        s5_lat, s5_ctx = s5_mixer(u_ctx, u_lat, s5_a_re[l], s5_a_im[l], s5_log_dt[l],
                                  s5_b_re[l], s5_b_im[l], s5_c_re[l], s5_c_im[l],
                                  s5_d[l], s5_w_glu[l], s5_b_glu[l], need_ctx, dtype)
        lru_lat, lru_ctx = rglru_mixer(r_ctx, q_ctx, r_lat, q_lat, rows,
                                       lru_conv_w[l], lru_conv_b[l], lru_w_a[l], lru_b_a[l],
                                       lru_w_x[l], lru_b_x[l], lru_lam[l], need_ctx, dtype)
        x = x + ga1 * (jnp.concatenate([s5_lat, lru_lat], axis=-1) @ w_out[l])

        if need_ctx:
            xc = xc + ga1c * (jnp.concatenate([s5_ctx, lru_ctx], axis=-1) @ w_out[l])
            hm = jnp.concatenate([modulate(rmsnorm(xc, norm2_g[l]), sh2c, sc2c),
                                  modulate(rmsnorm(x, norm2_g[l]), sh2, sc2)], axis=1)
            ym = hier_moe(hm, moe_w_group[l], moe_b_group[l], moe_w_router[l], moe_b_router[l],
                          moe_w1[l], moe_w3[l], moe_w2[l])
            xc = xc + ga2c * ym[:, :n_ctx]
            x = x + ga2 * ym[:, n_ctx:]
        else:
            hm = modulate(rmsnorm(x, norm2_g[l]), sh2, sc2)
            x = x + ga2 * hier_moe(hm, moe_w_group[l], moe_b_group[l], moe_w_router[l],
                                   moe_b_router[l], moe_w1[l], moe_w3[l], moe_w2[l])
    return rmsnorm(x, final_g)


_drawn_inputs = setup_inputs


def setup_inputs(seed=0):
    import zlib

    import numpy as np

    out = dict(_drawn_inputs(seed))
    spreads = {}
    factors = {'ctx': 2.689,
     'norm1_g': 4.957,
     'norm2_g': 6.455,
     's5_a_re': 64.0,
     's5_a_im': 13.052,
     's5_log_dt': 38.376,
     's5_b_re': 16.27,
     's5_b_im': 44.48,
     's5_c_re': 42.504,
     's5_c_im': 46.992,
     's5_b_glu': 21.732,
     'lru_b_a': 8.0,
     'lru_b_x': 8.0,
     'moe_b_group': 64.0,
     'moe_b_router': 8.0,
     'final_g': 8.348}
    for name, (base, spread) in spreads.items():
        noise = np.random.default_rng([zlib.crc32(name.encode()), seed]).standard_normal(out[name].shape)
        drawn = base * np.exp(spread * noise) if base else spread * noise
        out[name] = __import__('jax').numpy.asarray(drawn.astype(out[name].dtype))
    for name, factor in factors.items():
        out[name] = (out[name] * factor).astype(out[name].dtype)
    return out
```

```python
import math
from contextlib import ExitStack

import concourse.bass as bass
from concourse import mybir
from concourse.alu_op_type import AluOpType as ALU

ACT = mybir.ActivationFunctionType
AXX = mybir.AxisListType.X
F32 = mybir.dt.float32
I32 = mybir.dt.int32
U32 = mybir.dt.uint32

P = 128
D = 1024
KD = D // P
SEQ, CTX = 1024, 256
CH = 8
NL, NC_ = SEQ // CH, CTX // CH
NCH = NL + NC_
NTOK = SEQ + CTX
DS5, DLRU = 512, 512
GRP, GH, ST = 32, 16, 64
NQ, QG = 8, 4
EPS = 1e-6
NE, FE = 16, 512
ROWS, COLS = 16, 64
KB = 256

SM = {}
_at = 0
for _name, _w in (("c", 16), ("bmod", 16), ("g1", 8), ("are", 64), ("aim", 64), ("ldt", 64),
                  ("dsk", 32), ("bglu", 4), ("convw", 16), ("convb", 4), ("bgate", 16), ("lam", 8),
                  ("rbias", 20)):
    SM[_name] = (_at, _at + _w)
    _at += _w
NSM = _at


class Tally:

    def __init__(self, eng, sem):
        self.eng, self.sem, self.n = eng, sem, 0

    def did(self, ins):
        ins.then_inc(self.sem, 1)
        self.n += 1
        return self.n

    def wait(self):
        self.eng.wait_ge(self.sem, self.n)


def program(nc, t, out):
    with ExitStack() as ctx:
        def sem(name):
            return ctx.enter_context(nc.semaphore(name))

        arena = ctx.enter_context(nc.sbuf_tensor("arena", [P, 204 * KB], F32))
        sm = ctx.enter_context(nc.sbuf_tensor("small", [P, 984], F32))
        banks = [ctx.enter_context(nc.psum_tensor(f"bank{i}", [P, 512], F32)) for i in range(8)]

        def at(kb, *dims, parts=P):
            n = math.prod(dims)
            o = int(kb * KB)
            v = arena[0:parts, o:o + n]
            if len(dims) == 2:
                v = v.rearrange("p (a b) -> p a b", b=dims[1])
            if len(dims) == 3:
                v = v.rearrange("p (a b c) -> p a b c", b=dims[1], c=dims[2])
            if len(dims) == 4:
                v = v.rearrange("p (a b c d) -> p a b c d", b=dims[1], c=dims[2], d=dims[3])
            return v

        def small(name):
            return sm[:, SM[name][0]:SM[name][1]]

        xT = at(0, KD, NTOK)
        w_u, w_r, w_q = (at(40 + 16 * i, KD, 512) for i in range(3))
        wmod = [at(88 + 16 * i, KD, 512) for i in range(2)]
        xs = at(120, 8, D)
        xc = at(168, 2, D)
        junk = at(176, D)
        silu_bc = at(188, KD, P)
        utok = at(120, GRP, CH, GH)
        utokc = at(136, GRP, CH, GH)
        U = at(168, GRP, NCH)
        rows = at(152, 4, D)
        RPAD = 2 + CTX + 1 + 2 + SEQ + 1
        rS = at(120, 4, RPAD)
        gq = at(40, 4, SEQ)
        LAT0 = 2 + CTX + 1 + 2

        RL = RPAD - 3
        CL0 = CTX + 3
        zT = at(0, 4, SEQ)
        cosn, sinn = at(16, 8, NCH), at(21, 8, NCH)
        t1, t2 = at(26, 8, NCH), at(31, 8, NCH)
        uq = at(36, QG, NCH)
        bt = at(56, 8, CH, GH)
        ct, cs = at(60, 8, CH + 1, GH), at(64.5, 8, CH + 1, GH)
        ctmp = at(69, 8, CH + 1, GH)
        btT = at(73.5, 8, 192)
        wk = at(79.5, QG, 240, parts=GH)
        toep = at(83.25, QG, P)
        tr, ti = at(88, RL), at(93.0625, RL)
        la, sq = at(98.125, RL), at(103.1875, RL)
        xcv = at(108.25, RL)
        hf = at(113.5, SEQ)
        gh = at(140.25, 8, NCH)
        ctmp_d = at(149.5, QG, GH, parts=GH)
        zq = at(145.5, CH, P)
        p1, p2 = at(26, 8, NL), at(31, 8, NL)
        bcq = [at(188 + 2 * i, 4, P) for i in range(2)]
        wgm = at(201, 4, P)
        pwr, pwi = at(192, 64, 17), at(196.25, 64, 17)
        ph, phc, mag = at(152, 64, 17), at(156.25, 64, 17), at(160.5, 64, 17)
        pt = [at(164.75 + 0.25 * i, 64) for i in range(12)]

        s5T = at(16, 4, SEQ)
        wglu = at(32, 4, DS5)
        wout = at(88, KD, D)
        x2 = at(120, CH, D)
        h2 = at(168, CH, D)
        xt = [at(56 + 4 * i, D) for i in range(2)]
        h2T = [at(64 + 4 * i, KD, P) for i in range(2)]
        wr = at(72, KD, 20)
        g2row = at(76, D)
        junk3 = at(80, D)
        ltri, ones = at(84, P), at(84.5, P)
        lg = at(85, CH, 20)
        R1 = lambda i: at(85.625 + i * CH * 4 / KB, CH, 4)
        R3 = lambda i: at(73 + i * 0.5, CH, 16)
        RW = lambda i: at(86.75 + i * 16 / KB, 16)

        TT = 64
        MAXT = 2 * SEQ // TT + NE
        PADROW, TRASH = 2 * SEQ, 2 * SEQ + TT
        ew1 = [at(48 * i, KD, FE) for i in range(2)]
        ew3 = [at(48 * i + 16, KD, FE) for i in range(2)]
        ew2 = [at(48 * i + 32, 4, D) for i in range(2)]
        xg, ysb = at(96, D, parts=TT), at(106, D, parts=TT)
        xgT, sl, hT, yTs = at(100, KD, TT), at(102, 4, TT), at(103, 4, TT), at(104, KD, TT)
        y1, y2 = [at(168 + 4 * i, D) for i in range(2)], [at(176 + 4 * i, D) for i in range(2)]
        fin = [at(184 + 4 * i, D) for i in range(2)]
        gfrow, junk5 = at(192, D), at(196, D)
        xs_dram = nc.dram_tensor("tokens_by_expert", [2 * SEQ + TT, D], F32).ap()
        ys_dram = nc.dram_tensor("outputs_by_expert", [2 * SEQ + 2 * TT, D], F32).ap()

        o = NSM
        silu_c = sm[:, o:o + 16].rearrange("p (k v) -> p k v", v=2); o += 16
        shcol = sm[:, o:o + 16].rearrange("p (k v) -> p k v", v=2); o += 16
        sccol = sm[:, o:o + 16].rearrange("p (k v) -> p k v", v=2); o += 16
        ss = sm[:, o:o + 10]; o += 10
        rstd = sm[:, o:o + 10]; o += 10
        ident = sm[:, o:o + P]; o += P

        fi = sm[:, o:o + 64]; o += 64
        r8 = sm[:, o:o + 64]; o += 64
        n8 = sm[:, o:o + NCH]; o += NCH
        kx = sm[:, o:o + 34].rearrange("p (d k) -> p d k", k=17); o += 34
        n8i, kxi, fii = n8.bitcast(I32), kx.bitcast(I32), fi.bitcast(I32)
        sgn = sm[:, o:o + 2]; o += 2
        quarter = sm[:, o:o + 1].bitcast(I32); o += 1
        halfl, nhalfl = sm[:, o:o + 8], sm[:, o + 8:o + 16]; o += 16
        hbg = sm[:, o:o + 16]; o += 16
        assert o <= 984, o
        wsel = sm[:, 0:16].rearrange("p (k j) -> p k j", j=CH)
        slots = sm[:, 16:32].bitcast(U32)
        meta = sm[0:1, 32:32 + 64].bitcast(I32)
        rowtab = sm[0:1, 96:96 + MAXT + 3].bitcast(I32)
        ss3, rstd3 = sm[:, 160:168], sm[:, 168:176]
        ss5, rstd5 = sm[:, 176:184], sm[:, 184:192]
        TURN = 2.0 * math.pi * (1 - 2.0 ** -23) / 2.0 ** 32

        dm_small, dm_bc, dm_rowb = sem("dm_small"), sem("dm_bc"), sem("dm_rowb")
        dm_wmod = [sem(f"dm_wmod{i}") for i in range(2)]
        dm_x = [sem(f"dm_x{i}") for i in range(3)]
        dm_win = [sem(f"dm_win{i}") for i in range(3)]
        ident_ready = sem("ident_ready")
        silu_ready, silubc_ready = sem("silu_ready"), sem("silubc_ready")
        wmod_used = sem("wmod_used")
        ss_ready, ms_ready, sd_ready, xs_ready = sem("ss_ready"), sem("ms_ready"), sem("sd_ready"), sem("xs_ready")
        pe_job, act_evac, dve_evac = sem("pe_job"), sem("act_evac"), sem("dve_evac")
        act_self, dve_self, pool_self = sem("act_self"), sem("dve_self"), sem("pool_self")
        out_done = sem("out_done")
        pads_ready = sem("pads_ready")
        ints_ready, fi_ready, ph_ready, trig_ready, mag_in, dt_ready = (sem(n) for n in (
            "ints_ready", "fi_ready", "ph_ready", "trig_ready", "mag_in", "dt_ready"))
        sgn_ready = sem("sgn_ready")
        prep_done, sp_in, sp_exp = sem("prep_done"), sem("sp_in"), sem("sp_exp")

        jobs = [("modcol",)]
        for grp in range(3):
            jobs += [("xT", grp, k) for k in range(KD)]
        jobs += [("u", j) for j in range(10)]
        jobs += [("U", q, part) for q in range(NQ) for part in ("lat", "ctx")]
        rq = [("r", m, n) for m in range(4) for n in range(3)] + [("q", m, n) for m in range(4) for n in range(2)]
        mr = [("modrow", i) for i in range(8)]
        for i, job in enumerate(rq):
            jobs.append(job)
            if i % 2 == 1 and mr:
                jobs.append(mr.pop(0))
        jobs += mr

        def drainer(i, job):
            if job[0] in ("q",):
                return "act"
            if job[0] in ("modcol", "modrow"):
                return "dve"
            return ("act", "dve")[i % 2]

        plan, count = [], {"act": 0, "dve": 0}
        for i, job in enumerate(jobs):
            e = drainer(i, job)
            count[e] += 1
            plan.append((i, job, e, count[e]))
        evac = {"act": act_evac, "dve": dve_evac}
        place = {job: (i, e, n) for i, job, e, n in plan}

        def after_evac(eng, job):
            _, e, n = place[job]
            eng.wait_ge(evac[e], n)

        def tiles_of(grp):
            return (range(0, 4), range(4, 8), range(8, 10))[grp]

        def evacuate(eng, e, i, job, n):
            bank = banks[i % 8]
            done = evac[e]

            def copy(dst, src):
                if e == "act":
                    return nc.scalar.activation(dst, src, ACT.Copy)
                return nc.vector.tensor_copy(dst, src)

            kind = job[0]
            if kind == "xT":
                _, grp, k = job
                v = int(grp == 2)
                w = P * len(tiles_of(grp))
                dst = xT[:, k, 512 * grp:512 * grp + w]
                if e == "act":
                    ins = nc.scalar.activation(dst, bank[:, 0:w], ACT.Identity, bias=shcol[:, k, v:v + 1],
                                               scale=sccol[:, k, v:v + 1])
                else:
                    ins = nc.vector.tensor_scalar(dst, bank[:, 0:w], sccol[:, k, v:v + 1], shcol[:, k, v:v + 1],
                                                  ALU.mult, ALU.add)
            elif kind == "u":
                j = job[1]
                if j < 8:
                    ins = copy(utok[:, :, j], bank[:].rearrange("p (g h) -> p g h", h=GH))
                else:
                    for jq in range(4):
                        ins = copy(utokc[0:NC_, :, 4 * (j - 8) + jq],
                                   bank[32 * jq:32 * jq + 32, :].rearrange("p (g h) -> p g h", h=GH))
            elif kind == "U":
                _, q, part = job
                if part == "lat":
                    ins = copy(U[:, QG * q:QG * q + QG, NC_:NCH], bank[:].rearrange("p (g c) -> p g c", g=QG))
                else:
                    ins = copy(U[:, QG * q:QG * q + QG, 0:NC_], bank[:, 0:QG * NC_].rearrange("p (g c) -> p g c", g=QG))
            elif kind == "r":
                _, m, nn = job
                if nn == 2:
                    dst = rS[:, m, 2:2 + CTX].rearrange("p (c j) -> p j c", j=CH)
                    ins = copy(dst, bank[:, 0:CTX].rearrange("p (j c) -> p j c", j=CH))
                else:
                    v = rS[:, m, LAT0:LAT0 + SEQ].rearrange("p (cc j row) -> p j row cc", cc=8, j=8)[:, 4 * nn:4 * nn + 4]
                    src = bank[:].rearrange("p (j row cc) -> p j row cc", j=4, row=ROWS)
                    ins = copy(v, src)
            elif kind == "q":
                _, m, nn = job
                ins = nc.scalar.activation(gq[:, m, 512 * nn:512 * nn + 512], bank[:], ACT.Gelu_apprx_tanh)
            elif kind == "modrow":
                r = job[1]
                v = rows[:, r // 2, 512 * (r % 2):512 * (r % 2) + 512]
                if r == 0:
                    eng.wait_ge(dm_rowb, 16)
                ins = nc.vector.tensor_tensor(v, bank[:], v, ALU.add)
            ins.then_inc(done, 1)

        names2 = ("bt_ready", "ct_ready", "phase_ready", "turn_ready", "btp_ready", "btT_ready", "taps_ready",
                  "wk_ready", "uq_ready", "s_ready", "s_taken", "t_ready", "gh_ready", "pf_ready", "pb_ready", "y_ready",
                  "z_ready", "zp_ready", "zT_ready", "bt_used",
                  "xc_ready", "gate_ready", "gate_taken", "tri_ready", "decay_ready", "sqin_ready", "root_ready",
                  "b_ready", "a2_ready", "h_ready", "hs_done", "part_y")
        S2 = {n: sem(n) for n in names2}
        dm_bcq = [sem(f"dm_bcq{i}") for i in range(2)]
        dm_wgm, dm_toep = sem("dm_wgm"), sem("dm_toep")
        scan_ctx, scan_lat = sem("scan_ctx"), sem("scan_lat")
        dve2, pool2, act2 = sem("dve2"), sem("pool2"), sem("act2")
        NJ = len(jobs)
        GCH = ((0, 512), (512, 1024), (1024, RL))

        names3 = ("glu_job", "sig_ready", "s5T_ready", "out_job", "mul_ready", "x2_ready", "ss3_ready", "ms3_ready",
                  "sd3_ready", "hn_ready", "h2_ready", "h2T_job", "h2T_ready", "lg_job", "lg_ready", "a2row_ready",
                  "tri_built", "ex_in", "ex_out", "mask_ready", "rank_job", "slots_ready", "route_end", "zero_ready", "sgn3")
        S3 = {n: sem(n) for n in names3}
        dm_wglu, dm_wout, dm_wr, dm_g2, dm_pad = sem("dm_wglu"), sem("dm_wout"), sem("dm_wr"), sem("dm_g2"), sem("dm_pad")
        dm_xt = [sem(f"dm_xt{i}") for i in range(2)]
        dm_scat = sem("dm_scat")
        names4 = ("h_job", "sl_ready", "hT_ready", "yt_job", "y_evac", "xt_job", "xt_evac", "w2_job", "yt_copied")
        S4 = {n: sem(n) for n in names4}
        dm_w = [sem(f"dm_w{i}") for i in range(2)]
        dm_xg, dm_y, dm_gf = sem("dm_xg"), sem("dm_y"), sem("dm_gf")
        dm_g1y, dm_g2y = [sem(f"dm_g1y{i}") for i in range(2)], [sem(f"dm_g2y{i}") for i in range(2)]
        names5 = ("u1", "u2", "x3_ready", "ss5_ready", "ms5_ready", "sd5_ready", "o_ready")
        S5 = {n: sem(n) for n in names5}
        dm_out = [sem(f"dm_out{i}") for i in range(2)]

        class Steps:

            def __init__(self, eng, sem_, i, per, apart=False):
                self.apart = apart
                self.eng, self.sem, self.base, self.n, self.per = eng, sem_, i * per, 0, per

            def did(self, ins):
                ins.then_inc(self.sem, 1)
                self.n += 1

            def wait(self):
                self.eng.wait_ge(self.sem, self.base + self.n)
                if self.apart:
                    alone(self.eng)

            def end(self):
                assert self.n == self.per, self.n

        def alone(eng):
            eng.sem_inc(waits_passed[eng.engine], 1)

        def rev(ap_of, a, b):
            return ap_of[:, b - 1:(a - 1 if a else None):-1]

        def hn_sum(pool, j):
            pool.wait_ge(S3["hn_ready"], j + 1)
            nc.gpsimd.tensor_tensor(h2[:, j], h2[:, j], rows[:, 1], ALU.add).then_inc(S3["h2_ready"], 1)

        dve3 = sem("dve3")
        waits_passed = {eng.engine: sem(f"waits_passed{i}") for i, eng in enumerate((nc.sync, nc.gpsimd, nc.scalar, nc.tensor, nc.vector))}
        block = ctx.enter_context(nc.Block())

        @block.sync
        def _(sp):
            wm = t["w_mod"].rearrange("(k p) n -> p k n", p=P)
            win = t["w_in"].rearrange("(k p) n -> p k n", p=P)

            def load_wmod(c):
                if 2 <= c <= 4:
                    sp.wait_ge(wmod_used, c - 1)
                elif c == 5:
                    sp.wait_ge(pe_job, 1)
                elif c > 5:
                    sp.wait_ge(pe_job, place[("modrow", c - 6)][0] + 1)
                sp.dma_start(wmod[c % 2], wm[:, :, 512 * c:512 * c + 512]).then_inc(dm_wmod[c % 2], 16)

            sp.dma_start(sm[:, 0:NSM], t["smalls"]).then_inc(dm_small, 16)
            load_wmod(0)
            load_wmod(1)
            xv = t["x"].rearrange("(c j) d -> c j d", j=CH)
            sp.dma_start(xs[:, 0:4], xv[:, 0:4]).then_inc(dm_x[0], 16)
            sp.dma_start(xs[:, 4:8], xv[:, 4:8]).then_inc(dm_x[1], 16)
            sp.dma_start(xc, t["ctx"].rearrange("t p d -> p t d")).then_inc(dm_x[2], 16)
            load_wmod(2)
            load_wmod(3)
            for i, w in enumerate((w_u, w_r, w_q)):
                sp.dma_start(w, win[:, :, 512 * i:512 * i + 512]).then_inc(dm_win[i], 16)
            sp.wait_ge(prep_done, 1)
            sp.dma_start(rows, t["b_mod"][2 * D:6 * D].rearrange("(a n) -> a n", n=D).partition_broadcast(P)).then_inc(dm_rowb, 16)
            for c in range(4, 12):
                load_wmod(c)

            sp.wait_ge(pe_job, NJ)
            bcv = t["bc"].rearrange("p (a q n) -> p a q n", a=4, q=NQ)
            wgv = t["wg"].rearrange("p (m b n) -> p m b n", m=4, b=4)
            with sp.Fori(0, 4) as i:
                for s_ in range(2):
                    sp.wait_ge(S2["ct_ready"], 2 * i)
                    sp.dma_start(bcq[s_], bcv[:, :, bass.ds(2 * i + s_, 1), :].rearrange("p a q n -> p a (q n)")).then_inc(dm_bcq[s_], 16)
                sp.wait_ge(S2["gate_ready"], 12 * i)
                sp.dma_start(wgm, wgv[:, bass.ds(i, 1)].rearrange("p m b n -> p (m b) n")).then_inc(dm_wgm, 16)
                for s_ in range(2):
                    q = 2 * i + s_
                    sp.wait_ge(S2["wk_ready"], q + 1)
                    sp.wait_ge(S2["y_ready"], q)
                    for ji in range(CH):
                        sp.dma_start(toep[GH * ji:GH * ji + GH], wk[:, :, GH * (7 - ji):GH * (7 - ji) + P]).then_inc(dm_toep, 16)

            sp.wait_ge(S2["hs_done"], 4)
            sp.wait_ge(S2["zT_ready"], 8)
            sp.dma_start(wglu, t["w_glu"].rearrange("(k p) n -> p k n", p=P)).then_inc(dm_wglu, 16)
            for j in range(2):
                sp.dma_start(xt[j], xv[:, j]).then_inc(dm_xt[j], 16)
            sp.dma_start(g2row, t["g2"].partition_broadcast(P)).then_inc(dm_g2, 16)
            sp.dma_start(wr, t["w_router"].rearrange("(k p) n -> p k n", p=P)).then_inc(dm_wr, 16)
            sp.dma_start(wout, t["w_out"].rearrange("(k p) n -> p k n", p=P)).then_inc(dm_wout, 16)
            sp.wait_ge(S3["zero_ready"], 1)
            sp.dma_start(xs_dram[PADROW:PADROW + TT, :], junk3[0:TT]).then_inc(dm_pad, 16)
            for j in range(2, CH):
                sp.wait_ge(S3["x2_ready"], j - 1)
                sp.dma_start(xt[j % 2], xv[:, j]).then_inc(dm_xt[j % 2], 16)

            sp.wait_ge(S3["lg_job"], CH)
            w1v = t["w1"].rearrange("e (k p) f -> p e k f", p=P)
            w3v = t["w3"].rearrange("e (k p) f -> p e k f", p=P)
            w2v = t["w2"].rearrange("e (k p) d -> p e k d", p=P)

            def load_expert(e, s_):
                one = lambda v: v[:, bass.ds(e, 1)].rearrange("p e k f -> p (e k) f")
                sp.dma_start(ew1[s_], one(w1v)).then_inc(dm_w[s_], 16)
                sp.dma_start(ew3[s_], one(w3v)).then_inc(dm_w[s_], 16)
                sp.dma_start(ew2[s_], one(w2v)).then_inc(dm_w[s_], 16)
            load_expert(0, 0)
            sp.wait_ge(S3["route_end"], 1)
            load_expert(1, 1)
            with sp.Fori(1, NE // 2) as ep:
                for s_ in range(2):
                    free = sp.value_load(meta[:, bass.ds(2 * ep + s_ + 15, 1)], min_val=0, max_val=MAXT)
                    sp.wait_ge(S4["w2_job"], free)
                    load_expert(2 * ep + s_, s_)

            ov = out.rearrange("(c j) d -> c j d", j=CH)
            sp.dma_start(gfrow, t["gf"].partition_broadcast(P)).then_inc(dm_gf, 16)
            for j in range(CH):
                sp.wait_ge(S5["o_ready"], j + 1)
                sp.dma_start(ov[:, j], fin[j % 2]).then_inc(dm_out[j % 2], 16)
            for i in range(2):
                sp.wait_ge(dm_out[i], 16 * (CH // 2))

        @block.gpsimd
        def _(pool):
            pool.memset(ident, 0.0).then_inc(pool_self, 1)
            pool.wait_ge(pool_self, 1)
            pool.affine_select(out=ident, in_=ident, compare_op=ALU.not_equal, fill=1.0, base=0,
                               pattern=[[-1, P]], channel_multiplier=1).then_inc(ident_ready, 1)
            for d, (a, b, base, step) in ((0, (0, 9, 0, 1)), (0, (9, 17, 7, -1)), (1, (0, 9, 8, -1)), (1, (9, 17, 0, 1))):
                pool.iota(kxi[:, d, a:b], [[step, b - a]], base=base, channel_multiplier=0).then_inc(ints_ready, 1)
            pool.iota(n8i, [[CH, NCH]], base=0, channel_multiplier=0).then_inc(ints_ready, 1)
            pool.iota(quarter, [[0, 1]], base=1 << 30, channel_multiplier=0).then_inc(ints_ready, 1)
            pool.wait_ge(ints_ready, 6)
            pool.wait_ge(fi_ready, 1)
            phi, phci = ph.bitcast(I32), phc.bitcast(I32)
            for d in range(2):
                dst = phi.rearrange("p (q d g) k -> p q d g k", d=2, g=QG)[:, :, d]
                f = fii.rearrange("p (q d g) -> p q d g", d=2, g=QG)[:, :, d]
                for q in range(NQ):
                    nc.gpsimd.tensor_tensor(dst[:, q], f[:, q].unsqueeze(2).to_broadcast([P, QG, 17]),
                                            kxi[:, d].unsqueeze(1).to_broadcast([P, QG, 17]), ALU.mult).then_inc(pool_self, 1)
            pool.wait_ge(pool_self, 17)
            nc.gpsimd.tensor_tensor(phci, phi, quarter.unsqueeze(2).to_broadcast([P, 64, 17]), ALU.add).then_inc(ph_ready, 1)

            pool.wait_ge(pe_job, NJ)
            pool.wait_ge(prep_done, 1)
            g = nc.gpsimd
            shp = [P, 8, CH, GH]
            with pool.Fori(0, 4) as i:
                me = Steps(pool, pool2, i, 34, apart=True)

                def did(ins):
                    me.did(ins)
                    me.wait()

                for s_ in range(2):
                    q = 2 * i + s_
                    pool.wait_ge(dm_bcq[s_], 16 * (i + 1))
                    alone(pool)
                    X, Y = bcq[s_][:, 0].rearrange("p (a h) -> p a h", h=GH), bcq[s_][:, 1].rearrange("p (a h) -> p a h", h=GH)
                    CX, CY = bcq[s_][:, 2].rearrange("p (a h) -> p a h", h=GH), bcq[s_][:, 3].rearrange("p (a h) -> p a h", h=GH)
                    me.did(g.tensor_scalar(bcq[s_][:, 1], bcq[s_][:, 1], sgn[:, 0:1], None, ALU.mult))
                    me.did(g.tensor_scalar(bcq[s_][:, 2], bcq[s_][:, 2], sgn[:, 1:2], None, ALU.mult))
                    did(g.tensor_scalar(bcq[s_][:, 3], bcq[s_][:, 3], -1.0, None, ALU.mult))

                    def power(tab, a, n):
                        v = tab[:, bass.ds(8 * q, 8), a:a + n]
                        return v.unsqueeze(3).to_broadcast([P, 8, n, GH])

                    def over(x, n):
                        return x.unsqueeze(2).to_broadcast([P, 8, n, GH])
                    pool.wait_ge(S2["taps_ready"], q)
                    alone(pool)
                    me.did(g.tensor_tensor(bt, power(pwr, 9, 8), over(X, 8), ALU.mult))
                    did(g.tensor_tensor(ctmp[:, :, 0:8], power(pwi, 9, 8), over(Y, 8), ALU.mult))
                    did(g.tensor_tensor(bt, bt, ctmp[:, :, 0:8], ALU.add))
                    g.nop().then_inc(S2["bt_ready"], 1)
                    pool.wait_ge(S2["y_ready"], q)
                    alone(pool)
                    me.did(g.tensor_tensor(ct, power(pwr, 0, 9), over(CX, 9), ALU.mult))
                    did(g.tensor_tensor(ctmp, power(pwi, 0, 9), over(CY, 9), ALU.mult))
                    did(g.tensor_tensor(ct, ct, ctmp, ALU.add))
                    me.did(g.tensor_tensor(cs, power(pwr, 0, 9), over(CY, 9), ALU.mult))
                    did(g.tensor_tensor(ctmp, power(pwi, 0, 9), over(CX, 9), ALU.mult))
                    did(g.tensor_tensor(cs, cs, ctmp, ALU.subtract))
                    g.nop().then_inc(S2["ct_ready"], 1)
                    pool.wait_ge(S2["pf_ready"], q)
                    alone(pool)
                    ci, si = cosn.bitcast(I32), sinn.bitcast(I32)
                    f = fii[:, bass.ds(8 * q, 8)].unsqueeze(2).to_broadcast([P, 8, NCH])
                    did(g.tensor_tensor(si, f, n8i.unsqueeze(1).to_broadcast([P, 8, NCH]), ALU.mult))
                    g.tensor_tensor(ci, si, quarter.unsqueeze(2).to_broadcast([P, 8, NCH]), ALU.add).then_inc(S2["phase_ready"], 1)
                    pool.wait_ge(S2["decay_ready"], q + 1)
                    alone(pool)
                    pool.wait_ge(S2["h_ready"], q)
                    alone(pool)
                    g.tensor_tensor(sq, la, la, ALU.mult).then_inc(S2["a2_ready"], 1)
                    pool.wait_ge(S2["root_ready"], q + 1)
                    alone(pool)
                    pool.wait_ge(S2["b_ready"], q + 1)
                    alone(pool)
                    g.tensor_tensor(ti, ti, sq, ALU.mult).then_inc(S2["h_ready"], 1)
                    if s_ == 1:
                        pool.wait_ge(scan_lat, q + 1)
                        alone(pool)
                        did(g.tensor_tensor(hf, hf, ti[:, CL0:RL], ALU.add))
                        v = gq[:, bass.ds(i, 1)].rearrange("p m (j row cc) -> p (m j) row cc", j=CH, row=ROWS)
                        hv = hf.rearrange("p (cc j row) -> p j row cc", cc=8, j=CH)
                        for j in range(CH):
                            ins = g.tensor_tensor(v[:, j], v[:, j], hv[:, j], ALU.mult)
                            if j < CH - 1:
                                me.did(ins)
                        ins.then_inc(S2["hs_done"], 1)
                me.end()

            pool.wait_ge(S2["hs_done"], 4)
            pool.wait_ge(S2["zT_ready"], 8)
            g.memset(junk3, 0.0).then_inc(S3["zero_ready"], 1)
            g.memset(ones, 1.0).then_inc(pool_self, 1)
            pool.wait_ge(pool_self, 18)
            g.affine_select(out=ltri, in_=ones, compare_op=ALU.is_gt, fill=0.0, base=0,
                            pattern=[[1, P]], channel_multiplier=-1).then_inc(S3["tri_built"], 1)
            for j in range(CH):
                pool.wait_ge(S3["mul_ready"], 2 * j + 2)
                pool.wait_ge(dm_xt[j % 2], 16 * (j // 2 + 1))
                g.tensor_tensor(x2[:, j], x2[:, j], xt[j % 2], ALU.add).then_inc(S3["x2_ready"], 1)
                if j:
                    hn_sum(pool, j - 1)
            hn_sum(pool, CH - 1)
            pool.wait_ge(S3["slots_ready"], 1)
            pool.wait_ge(S3["h2_ready"], CH)
            for k in range(2):
                for j in range(CH):
                    c0 = CH * k + j
                    g.indirect_dma_start(xs_dram[0:2 * SEQ, :], bass.IndirectOffsetOnAxis(ap=slots[:, c0:c0 + 1], axis=0),
                                         h2[:, j], None).then_inc(dm_scat, 16)
            pool.wait_ge(dm_scat, 16 * 2 * CH)
            pool.wait_ge(dm_pad, 16)
            pool.wait_ge(S3["route_end"], 1)
            g.dma_start(xg, xs_dram[0:TT, :]).then_inc(dm_xg, 16)
            with pool.Fori(0, NE) as e:
                a = pool.value_load(meta[:, bass.ds(e, 1)], min_val=0, max_val=MAXT)
                b = pool.value_load(meta[:, bass.ds(e + 1, 1)], min_val=1, max_val=MAXT)
                with pool.Fori(a, b) as n:
                    row = pool.value_load(rowtab[:, bass.ds(n + 2, 1)], min_val=0, max_val=PADROW)
                    pool.wait_ge(S4["xt_job"], n + 1)
                    alone(pool)
                    g.dma_start(xg, xs_dram[bass.ds(row, TT), :]).then_inc(dm_xg, 16)
                    orow = pool.value_load(rowtab[:, bass.ds(n, 1)], min_val=0, max_val=TRASH)
                    pool.wait_ge(S4["y_evac"], 2 * n + 2)
                    pool.wait_ge(dm_y, 16 * n)
                    alone(pool)
                    g.dma_start(ys_dram[bass.ds(orow, TT), :], ysb).then_inc(dm_y, 16)
            last = pool.value_load(meta[:, NE:NE + 1], min_val=1, max_val=MAXT)
            orow = pool.value_load(rowtab[:, bass.ds(last, 1)], min_val=0, max_val=TRASH)
            pool.wait_ge(S4["y_evac"], 2 * last + 2)
            pool.wait_ge(dm_y, 16 * last)
            alone(pool)
            g.dma_start(ys_dram[bass.ds(orow, TT), :], ysb).then_inc(dm_y, 16)
            pool.wait_ge(dm_y, 16 * last + 16)
            pool.wait_ge(dm_xg, 16 * last + 16)
            alone(pool)
            for j in range(CH):
                if j >= 2:
                    pool.wait_ge(S5["u2"], j - 1)
                g.indirect_dma_start(y1[j % 2], None, ys_dram[0:2 * SEQ, :], bass.IndirectOffsetOnAxis(ap=slots[:, j:j + 1], axis=0)).then_inc(dm_g1y[j % 2], 16)
                g.indirect_dma_start(y2[j % 2], None, ys_dram[0:2 * SEQ, :], bass.IndirectOffsetOnAxis(ap=slots[:, CH + j:CH + j + 1], axis=0)).then_inc(dm_g2y[j % 2], 16)

        @block.scalar
        def _(act):
            me = Tally(act, act_self)
            act.wait_ge(dm_small, 16)
            nc.scalar.activation(silu_c, small("c").rearrange("p (k v) -> p k v", v=2), ACT.Sigmoid).then_inc(silu_ready, 1)
            nc.scalar.activation(pt[0], small("ldt"), ACT.Exp).then_inc(dt_ready, 1)
            act.wait_ge(sp_in, 1)
            nc.scalar.activation(pt[11][:, 8:16], pt[11][:, 0:8], ACT.Exp).then_inc(sp_exp, 1)
            for grp in range(3):
                act.wait_ge(dm_x[grp], 16)
                for i in tiles_of(grp):
                    src = xs[:, i] if i < 8 else xc[:, i - 8]
                    ins = nc.scalar.activation(junk, src, ACT.Square, accum_out=ss[:, i:i + 1])
                    me.did(ins)
                    me.wait()
                nc.scalar.nop().then_inc(ss_ready, 1)
                act.wait_ge(ms_ready, grp + 1)
                a, b = tiles_of(grp)[0], tiles_of(grp)[-1] + 1
                nc.scalar.activation(rstd[:, a:b], ss[:, a:b], ACT.Sqrt).then_inc(sd_ready, 1)

            act.wait_ge(ph_ready, 1)
            me.did(nc.scalar.activation(ph, ph.bitcast(I32), ACT.Sin, scale=TURN))
            me.did(nc.scalar.activation(phc, phc.bitcast(I32), ACT.Sin, scale=TURN))
            act.wait_ge(mag_in, 1)
            me.wait()
            nc.scalar.activation(mag, mag, ACT.Exp).then_inc(trig_ready, 1)
            for i, job, e, n in plan:
                if e != "act":
                    continue
                act.wait_ge(pe_job, i + 1)
                evacuate(act, "act", i, job, n)

            act.wait_ge(pe_job, NJ)
            A = nc.scalar.activation
            with act.Fori(0, 4) as i:
                me = Steps(act, act2, i, 6)
                for s_ in range(2):
                    q = 2 * i + s_
                    act.wait_ge(S2["y_ready"], q)
                    alone(act)
                    A(uq, U[:, bass.ds(QG * q, QG), :], ACT.Copy).then_inc(S2["uq_ready"], 1)
                    for b in range(2):
                        act.wait_ge(S2["btp_ready"], 2 * q + b + 1)
                        src = banks[3 + b][:].rearrange("p (g n) -> p g n", n=P)
                        me.did(A(btT[:, 4 * b:4 * b + 4, 0:P], src, ACT.Copy))
                        A(btT[:, 4 * b:4 * b + 4, P:192], src[:, :, 0:ST], ACT.Copy, scale=-1.0).then_inc(S2["btT_ready"], 1)
                    act.wait_ge(S2["phase_ready"], q + 1)
                    me.did(A(sinn, sinn.bitcast(I32), ACT.Sin, scale=TURN))
                    A(cosn, cosn.bitcast(I32), ACT.Sin, scale=TURN).then_inc(S2["turn_ready"], 1)
                    act.wait_ge(S2["gate_taken"], q)
                    for gi in range(6):
                        gate, ch = gi // 3, gi % 3
                        act.wait_ge(S2["gate_ready"], 6 * q + gi + 1)
                        a, b = GCH[ch]
                        bias = hbg.rearrange("p (b m) -> p b m", m=4)[:, 2 * s_ + gate, bass.ds(i, 1)]
                        alone(act)
                        A((tr, ti)[gate][:, a:b], banks[gi % 3][:, 0:b - a], ACT.Tanh, bias=bias, scale=0.5).then_inc(S2["tri_ready"], 1)
                    act.wait_ge(S2["tri_ready"], 6 * q + 6)
                    lcol = lambda x: x.rearrange("p (d m) -> p d m", m=4)[:, s_, bass.ds(i, 1)]
                    alone(act)
                    A(la, tr, ACT.Exp, bias=lcol(halfl), scale=lcol(halfl)).then_inc(S2["decay_ready"], 1)
                    alone(act)
                    A(tr, tr, ACT.Tanh, bias=lcol(nhalfl), scale=lcol(nhalfl)).then_inc(S2["sqin_ready"], 1)
                    act.wait_ge(S2["part_y"], q + 1)
                    A(sq, sq, ACT.Sqrt, scale=0.25).then_inc(S2["root_ready"], 1)
                    act.wait_ge(S2["y_ready"], q + 1)
                    if s_ == 0:
                        act.wait_ge(S2["zp_ready"], 2 * i)
                    for jo in range(1):
                        A(zq[:, :, 64 * s_:64 * s_ + 64].rearrange("p j (g h) -> p g j h", h=GH),
                          banks[7][:].rearrange("p (g j h) -> p g j h", g=QG, j=CH), ACT.Gelu_apprx_tanh).then_inc(S2["z_ready"], 1)
                for b in range(2):
                    act.wait_ge(S2["zp_ready"], 2 * i + b + 1)
                    alone(act)
                    A(zT[:, bass.ds(i, 1), 512 * b:512 * b + 512].rearrange("p a n -> p (a n)"), banks[5 + b][:], ACT.Copy).then_inc(S2["zT_ready"], 1)
                me.end()

            act.wait_ge(S2["zT_ready"], 8)
            for n in range(8):
                m, h = n // 2, n % 2
                act.wait_ge(S3["glu_job"], n + 1)
                A(s5T[:, m, 512 * h:512 * h + 512], banks[n % 2][:], ACT.Sigmoid, bias=small("bglu")[:, m:m + 1]).then_inc(S3["sig_ready"], 1)
            for j in range(CH + 1):
                if j < CH:
                    act.wait_ge(S3["x2_ready"], j + 1)
                    if j == 0:
                        act.wait_ge(dm_pad, 16)
                    else:
                        act.wait_ge(S3["ss3_ready"], j)
                    A(junk3, x2[:, j], ACT.Square, accum_out=ss3[:, j:j + 1]).then_inc(S3["ss3_ready"], 1)
                    act.wait_ge(S3["ms3_ready"], j + 1)
                    A(rstd3[:, j:j + 1], ss3[:, j:j + 1], ACT.Sqrt).then_inc(S3["sd3_ready"], 1)
                if j:
                    for b in range(2):
                        act.wait_ge(S3["h2T_job"], 2 * j - 1 + b)
                        if j >= 3:
                            act.wait_ge(S3["lg_job"], j - 2)
                        A(h2T[(j - 1) % 2][:, 4 * b:4 * b + 4], banks[6 + b][:].rearrange("p (k n) -> p k n", n=P), ACT.Copy).then_inc(S3["h2T_ready"], 1)
            for n in range(2):
                act.wait_ge(S3["ex_in"], n + 1)
                v_ = (R1(0), at(85.625 + 5 * CH * 4 / KB, CH))[n]
                A(v_, v_, ACT.Exp).then_inc(S3["ex_out"], 1)
            act.wait_ge(S3["route_end"], 1)
            act.wait_ge(S4["xt_job"], 1)
            A(xgT, banks[4][:].rearrange("p (k n) -> p k n", n=TT), ACT.Copy).then_inc(S4["xt_evac"], 1)
            with act.Fori(0, NE) as e:
                a = act.value_load(meta[:, bass.ds(e, 1)], min_val=0, max_val=MAXT)
                b = act.value_load(meta[:, bass.ds(e + 1, 1)], min_val=1, max_val=MAXT)
                with act.Fori(a, b) as n:
                    act.wait_ge(S4["hT_ready"], 4 * n)
                    for f in range(4):
                        act.wait_ge(S4["h_job"], 4 * n + f + 1)
                        A(sl[:, f], banks[f][:, 0:TT], ACT.Silu).then_inc(S4["sl_ready"], 1)
                    act.wait_ge(dm_y, 16 * n)
                    for h in range(2):
                        act.wait_ge(S4["yt_job"], 2 * n + h + 1)
                        A(ysb[:, 512 * h:512 * h + 512], banks[6 + h][0:TT, :], ACT.Copy).then_inc(S4["y_evac"], 1)
                    act.wait_ge(S4["xt_job"], n + 2)
                    A(xgT, banks[4][:].rearrange("p (k n) -> p k n", n=TT), ACT.Copy).then_inc(S4["xt_evac"], 1)
            last = act.value_load(meta[:, NE:NE + 1], min_val=1, max_val=MAXT)
            act.wait_ge(dm_y, 16 * last)
            for h in range(2):
                act.wait_ge(S4["yt_job"], 2 * last + h + 1)
                A(ysb[:, 512 * h:512 * h + 512], banks[6 + h][0:TT, :], ACT.Copy).then_inc(S4["y_evac"], 1)
            for j in range(CH):
                act.wait_ge(S5["x3_ready"], j + 1)
                if j:
                    act.wait_ge(S5["ss5_ready"], j)
                A(junk5, fin[j % 2], ACT.Square, accum_out=ss5[:, j:j + 1]).then_inc(S5["ss5_ready"], 1)
                act.wait_ge(S5["ms5_ready"], j + 1)
                A(rstd5[:, j:j + 1], ss5[:, j:j + 1], ACT.Sqrt).then_inc(S5["sd5_ready"], 1)

        ROUND = 1.5 * 2.0 ** 23

        def powers_phase(dve, me):
            v = nc.vector

            def did(ins):
                me.did(ins)
                me.wait()

            lam = small("lam")
            e8, w, s8, s2, p8 = pt[11][:, 0:8], pt[11][:, 8:16], pt[11][:, 16:24], pt[11][:, 24:32], pt[11][:, 32:40]
            did(v.tensor_scalar(e8, lam, -1.0, None, ALU.mult))
            v.tensor_tensor(e8, lam, e8, ALU.min).then_inc(sp_in, 1)
            dve.wait_ge(sp_exp, 1)
            did(v.tensor_scalar(s8, w, 2.0, None, ALU.add))
            did(v.reciprocal(s8, s8))
            did(v.tensor_tensor(s8, s8, w, ALU.mult))
            did(v.tensor_tensor(s2, s8, s8, ALU.mult))
            did(v.tensor_scalar(p8, s2, 1.0 / 17, 1.0 / 15, ALU.mult, ALU.add))
            for c in (13, 11, 9, 7, 5, 3, 1):
                did(v.tensor_tensor(p8, p8, s2, ALU.mult))
                did(v.tensor_scalar(p8, p8, 1.0 / c, None, ALU.add))
            did(v.scalar_tensor_tensor(p8, p8, 2.0, s8, ALU.mult, ALU.mult))
            did(v.tensor_scalar(s8, lam, -1.0, 0.0, ALU.mult, ALU.max))
            did(v.tensor_tensor(p8, p8, s8, ALU.add))
            did(v.tensor_scalar(halfl, p8, -4.0, None, ALU.mult))
            did(v.tensor_scalar(nhalfl, p8, 4.0, None, ALU.mult))
            did(v.tensor_scalar(hbg, small("bgate"), 0.5, None, ALU.mult))

            dt, th, er, kk, r = pt[0], pt[1], pt[2], pt[3], pt[4]
            dve.wait_ge(dt_ready, 1)
            did(v.tensor_tensor(th, small("aim"), dt, ALU.mult))
            did(v.tensor_tensor(er, small("are"), dt, ALU.mult))
            did(v.tensor_scalar(kk, th, 1 / (2 * math.pi), ROUND, ALU.mult, ALU.add))
            did(v.tensor_scalar(kk, kk, -ROUND, None, ALU.add))
            parts, rest = [], 2 * math.pi
            for bits in (5, 16):
                parts.append(math.floor(rest * 2 ** bits) / 2 ** bits)
                rest -= parts[-1]
            did(v.scalar_tensor_tensor(r, kk, -parts[0], th, ALU.mult, ALU.add))
            did(v.scalar_tensor_tensor(r, kk, -parts[1], r, ALU.mult, ALU.add))
            did(v.scalar_tensor_tensor(r, kk, -rest, r, ALU.mult, ALU.add))
            did(v.tensor_scalar(r, r, 2.0 ** 32 / (2 * math.pi), 2147483520.0, ALU.mult, ALU.min))
            v.tensor_scalar(fii, r, -2147483520.0, None, ALU.max).then_inc(fi_ready, 1)
            dve.wait_ge(ints_ready, 6)
            for d in range(2):
                dst = mag.rearrange("p (q d g) k -> p q d g k", d=2, g=QG)[:, :, d]
                e = er.rearrange("p (q d g) -> p q d g", d=2, g=QG)[:, :, d]
                for q in range(NQ):
                    ins = v.tensor_tensor(dst[:, q], e[:, q].unsqueeze(2).to_broadcast([P, QG, 17]),
                                          kxi[:, d].unsqueeze(1).to_broadcast([P, QG, 17]), ALU.mult)
            ins.then_inc(mag_in, 1)
            den, tmp = pt[5], pt[6]
            did(v.tensor_tensor(den, small("are"), small("are"), ALU.mult))
            did(v.tensor_tensor(tmp, small("aim"), small("aim"), ALU.mult))
            did(v.tensor_tensor(den, den, tmp, ALU.add))
            did(v.reciprocal(den, den))

        def powers_tables(dve, me):
            v = nc.vector

            def did(ins):
                me.did(ins)
                me.wait()
            dve.wait_ge(trig_ready, 1)
            me.did(v.tensor_tensor(pwr, phc, mag, ALU.mult))
            did(v.tensor_tensor(pwi, ph, mag, ALU.mult))
            den, nr, ni, wr, wi, tmp = pt[5], pt[6], pt[7], pt[8], pt[9], pt[10]
            by_d = lambda x: x.rearrange("p (q d g) -> p d q g", d=2, g=QG)
            pw_d = lambda x: x.rearrange("p (q d g) k -> p d q g k", d=2, g=QG)
            for d, one, eight in ((0, 1, 8), (1, 7, 0)):
                me.did(v.tensor_scalar(by_d(nr)[:, d], pw_d(pwr)[:, d, :, :, one], -1.0, None, ALU.add))
                me.did(v.tensor_copy(by_d(ni)[:, d], pw_d(pwi)[:, d, :, :, one]))
                me.did(v.tensor_copy(by_d(r8)[:, d], pw_d(mag)[:, d, :, :, eight]))
            me.wait()
            are, aim = small("are"), small("aim")
            did(v.tensor_tensor(wr, nr, are, ALU.mult))
            did(v.tensor_tensor(tmp, ni, aim, ALU.mult))
            did(v.tensor_tensor(wr, wr, tmp, ALU.add))
            did(v.tensor_tensor(wr, wr, den, ALU.mult))
            did(v.tensor_tensor(wi, ni, are, ALU.mult))
            did(v.tensor_tensor(tmp, nr, aim, ALU.mult))
            did(v.tensor_tensor(wi, wi, tmp, ALU.subtract))
            did(v.tensor_tensor(wi, wi, den, ALU.mult))
            b = lambda x: x.unsqueeze(2).to_broadcast([P, 64, 8])
            pr, pi_ = pwr[:, :, 9:17], pwi[:, :, 9:17]
            x1, x2, x3 = ph[:, :, 0:8], phc[:, :, 0:8], mag[:, :, 0:8]
            me.did(v.tensor_tensor(x1, pr, b(wr), ALU.mult))
            me.did(v.tensor_tensor(x2, pi_, b(wi), ALU.mult))
            did(v.tensor_tensor(x3, pr, b(wi), ALU.mult))
            did(v.tensor_tensor(pr, x1, x2, ALU.subtract))
            did(v.tensor_tensor(x1, pi_, b(wr), ALU.mult))
            v.tensor_tensor(pi_, x3, x1, ALU.add).then_inc(prep_done, 1)

        @block.vector
        def _(dve):
            me = Tally(dve, dve_self)
            dve.wait_ge(silu_ready, 1)
            cv = small("c").rearrange("p (k v) -> p k v", v=2)
            me.did(nc.vector.tensor_tensor(silu_c, silu_c, cv, ALU.mult))
            me.wait()
            nc.vector.tensor_copy(silu_bc, silu_c[:, :, 0:1].to_broadcast([P, KD, P])).then_inc(silubc_ready, 1)

            nc.vector.memset(sgn[0:ST, 0:1], -1.0)
            nc.vector.memset(sgn[ST:P, 0:1], 1.0)
            nc.vector.memset(sgn[0:ST, 1:2], 1.0)
            nc.vector.memset(sgn[ST:P, 1:2], -1.0).then_inc(sgn_ready, 1)
            powers_phase(dve, me)
            dve.wait_ge(pe_job, 1)
            bm = small("bmod")
            mc = banks[0][:, 0:32].rearrange("p (m v) -> p m v", v=2)
            me.did(nc.vector.tensor_tensor(shcol, mc[:, 0:8], bm[:, 0:8].unsqueeze(2).to_broadcast([P, 8, 2]), ALU.add))
            me.did(nc.vector.tensor_tensor(sccol, mc[:, 8:16], bm[:, 8:16].unsqueeze(2).to_broadcast([P, 8, 2]), ALU.add))
            me.wait()
            me.did(nc.vector.scalar_tensor_tensor(sccol, sccol, 1.0, small("g1").unsqueeze(2).to_broadcast([P, 8, 2]),
                                                  ALU.add, ALU.mult))
            me.wait()
            nc.vector.nop().then_inc(dve_evac, 1)

            for grp in range(3):
                dve.wait_ge(ss_ready, grp + 1)
                a, b = tiles_of(grp)[0], tiles_of(grp)[-1] + 1
                nc.vector.tensor_scalar(ss[:, a:b], ss[:, a:b], 1.0 / D, EPS, ALU.mult, ALU.add).then_inc(ms_ready, 1)
                dve.wait_ge(sd_ready, grp + 1)
                me.did(nc.vector.reciprocal(rstd[:, a:b], rstd[:, a:b]))
                me.wait()
                for i in tiles_of(grp):
                    v = xs[:, i] if i < 8 else xc[:, i - 8]
                    ins = nc.vector.tensor_scalar(v, v, rstd[:, i:i + 1], None, ALU.mult)
                ins.then_inc(xs_ready, 1)

            powers_tables(dve, me)
            for i, job, e, n in plan[1:]:
                if e != "dve":
                    continue
                dve.wait_ge(pe_job, i + 1)
                evacuate(dve, "dve", i, job, n)

            dve.wait_ge(pe_job, NJ)
            v = nc.vector
            for m in range(4):
                v.memset(rS[:, m, 0:2], 0.0)
                v.memset(rS[:, m, 2 + CTX:LAT0], 0.0)
                ins = v.memset(rS[:, m, RPAD - 1:RPAD], 0.0)
            ins.then_inc(pads_ready, 1)
            dve.wait_ge(pads_ready, 1)
            cw = small("convw").rearrange("p (m k) -> p m k", k=4)
            dsk = sm[0:GH, SM["dsk"][0]:SM["dsk"][1]]
            with dve.Fori(0, 4) as i:
                me = Steps(dve, dve2, i, 28)

                def did(ins):
                    me.did(ins)
                    me.wait()

                r = lambda k: rS[:, bass.ds(i, 1), k:k + RL].rearrange("p a n -> p (a n)")
                w = lambda k: cw[:, bass.ds(i, 1), k:k + 1].rearrange("p a n -> p (a n)")
                dve.wait_ge(S2["gate_ready"], 12 * i)
                dve.wait_ge(S2["b_ready"], 2 * i)
                did(v.tensor_scalar(xcv, r(0), w(0), small("convb")[:, bass.ds(i, 1)], ALU.mult, ALU.add))
                did(v.scalar_tensor_tensor(xcv, r(1), w(1), xcv, ALU.mult, ALU.add))
                did(v.scalar_tensor_tensor(xcv, r(2), w(2), xcv, ALU.mult, ALU.add))
                did(v.scalar_tensor_tensor(xcv, r(3), w(3), xcv, ALU.mult, ALU.add))
                v.nop().then_inc(S2["xc_ready"], 1)
                for s_ in range(2):
                    q = 2 * i + s_
                    for b in range(2):
                        dve.wait_ge(S2["taps_ready"], q + 1)
                        if b == 0:
                            dve.wait_ge(dm_toep, 128 * q)
                        me.did(v.tensor_copy(wk[:, 2 * b:2 * b + 2], banks[5 + b][0:GH, 0:480].rearrange("p (g n) -> p g n", n=240)))
                    eye = ident[0:GH, 0:GH].unsqueeze(1).to_broadcast([GH, QG, GH])
                    did(v.tensor_tensor(ctmp_d, eye, dsk[:, bass.ds(QG * q, QG)].unsqueeze(2).to_broadcast([GH, QG, GH]), ALU.mult))
                    v.tensor_tensor(wk[:, :, 112:128], wk[:, :, 112:128], ctmp_d, ALU.add).then_inc(S2["wk_ready"], 1)
                    dve.wait_ge(S2["turn_ready"], q + 1)
                    dve.wait_ge(S2["y_ready"], q)
                    for pr in range(4):
                        g0 = 2 * pr
                        for part, (tab, dst) in enumerate(((cosn, t1), (sinn, t2))):
                            bank = banks[3 + (2 * pr + part) % 4]
                            dve.wait_ge(S2["s_ready"], 8 * q + 2 * pr + part + 1)
                            src = bank[:, 0:2 * NCH].rearrange("p (g n) -> p g n", n=NCH)
                            if g0 < 4:
                                ins = v.tensor_tensor(dst[:, g0:g0 + 2], src, tab[:, g0:g0 + 2], ALU.mult)
                            else:
                                me.did(v.tensor_tensor(dst[:, g0:g0 + 2, 0:NC_], src[:, :, NC_ - 1::-1], tab[:, g0:g0 + 2, 0:NC_], ALU.mult))
                                ins = v.tensor_tensor(dst[:, g0:g0 + 2, NC_:NCH], src[:, :, NCH - 1:NC_ - 1:-1], tab[:, g0:g0 + 2, NC_:NCH], ALU.mult)
                            ins.then_inc(S2["s_taken"], 1)
                    dve.wait_ge(S2["s_taken"], 8 * q + 8)
                    me.wait()
                    did(v.tensor_tensor(t1, t1, t2, ALU.add))
                    for g in range(8):
                        ins = v.tensor_tensor_scan(gh[:, g], r8[:, bass.ds(8 * q + g, 1)].to_broadcast([P, NCH]), t1[:, g], 0.0, ALU.mult, ALU.add)
                    did(ins)
                    for tab, dst in ((cosn, p1), (sinn, p2)):
                        me.did(v.tensor_tensor(dst[:, 0:4], gh[:, 0:4, NC_ - 1:NCH - 1], tab[:, 0:4, NC_ - 1:NCH - 1], ALU.mult))
                        ins = v.tensor_tensor(dst[:, 4:8, ::-1], gh[:, 4:8, NC_ - 1:NCH - 1], tab[:, 4:8, NC_ - 1:NCH - 1], ALU.mult)
                        if tab is cosn:
                            me.did(ins)
                    ins.then_inc(S2["pf_ready"], 1)
                    dve.wait_ge(S2["tri_ready"], 6 * q + 6)
                    v.scalar_tensor_tensor(ti, ti, 1.0, xcv, ALU.add, ALU.mult).then_inc(S2["b_ready"], 1)
                    dve.wait_ge(S2["sqin_ready"], q + 1)
                    dve.wait_ge(S2["a2_ready"], q + 1)
                    v.scalar_tensor_tensor(sq, sq, 1.0, tr, ALU.add, ALU.mult).then_inc(S2["part_y"], 1)
                    dve.wait_ge(S2["h_ready"], q + 1)
                    if s_ == 0:
                        dve.wait_ge(S2["hs_done"], i)
                        v.tensor_tensor_scan(ti[:, 0:CTX], la[:, 0:CTX], ti[:, 0:CTX], 0.0, ALU.mult, ALU.add).then_inc(scan_ctx, 1)
                        dve.wait_ge(scan_ctx, q + 1)
                        v.tensor_tensor_scan(hf, la[:, CL0:RL], ti[:, CL0:RL], ti[:, CTX - 1:CTX], ALU.mult, ALU.add).then_inc(scan_lat, 1)
                        dve.wait_ge(scan_lat, q + 1)
                        v.nop().then_inc(S2["gate_taken"], 1)
                    else:
                        c_ = rev(ti, 0, CTX)
                        v.tensor_tensor_scan(c_, rev(la, 0, CTX), c_, 0.0, ALU.mult, ALU.add).then_inc(scan_ctx, 1)
                        dve.wait_ge(scan_ctx, q + 1)
                        l_ = rev(ti, CL0, RL)
                        v.tensor_tensor_scan(l_, rev(la, CL0, RL), l_, ti[:, 0:1], ALU.mult, ALU.add).then_inc(scan_lat, 1)
                        dve.wait_ge(S2["hs_done"], i + 1)
                        v.nop().then_inc(S2["gate_taken"], 1)
                me.end()

            dve.wait_ge(S2["zT_ready"], 8)
            dve.wait_ge(S2["hs_done"], 4)
            me = Tally(dve, dve3)

            def did(ins):
                me.did(ins)
                me.wait()
            dve.wait_ge(dm_g2, 16)
            did(v.scalar_tensor_tensor(rows[:, 2], rows[:, 2], 1.0, g2row, ALU.add, ALU.mult))
            for n in range(8):
                m, h = n // 2, n % 2
                dve.wait_ge(S3["sig_ready"], n + 1)
                w_ = s5T[:, m, 512 * h:512 * h + 512]
                v.tensor_tensor(w_, w_, zT[:, m, 512 * h:512 * h + 512], ALU.mult).then_inc(S3["s5T_ready"], 1)

            def norm(j):
                dve.wait_ge(S3["ss3_ready"], j + 1)
                v.tensor_scalar(ss3[:, j:j + 1], ss3[:, j:j + 1], 1.0 / D, EPS, ALU.mult, ALU.add).then_inc(S3["ms3_ready"], 1)
                dve.wait_ge(S3["sd3_ready"], j + 1)
                did(v.reciprocal(rstd3[:, j:j + 1], rstd3[:, j:j + 1]))
                v.scalar_tensor_tensor(h2[:, j], x2[:, j], rstd3[:, j:j + 1], rows[:, 2], ALU.mult, ALU.mult).then_inc(S3["hn_ready"], 1)

            def logits(j):
                dve.wait_ge(S3["lg_job"], j + 1)
                v.tensor_tensor(lg[:, j], banks[j % 2][:, 0:20], small("rbias"), ALU.add).then_inc(S3["lg_ready"], 1)
            for j in range(CH + 2):
                if j < CH:
                    for h in range(2):
                        dve.wait_ge(S3["out_job"], 2 * j + h + 1)
                        v.tensor_tensor(x2[:, j, 512 * h:512 * h + 512], banks[2 + (2 * j + h) % 4][:],
                                        rows[:, 0, 512 * h:512 * h + 512], ALU.mult).then_inc(S3["mul_ready"], 1)
                if 1 <= j <= CH:
                    norm(j - 1)
                if j >= 2:
                    logits(j - 2)
            dve.wait_ge(S3["lg_ready"], CH)

            bj = lambda x, n: x.unsqueeze(2).to_broadcast([P, CH, n])
            iota4 = RW(0)[:, 0:4].unsqueeze(1).to_broadcast([P, CH, 4])
            for k in range(4):
                me.did(v.memset(RW(0)[:, k:k + 1], float(k - 8)))
            me.did(v.memset(RW(4), 1.0))
            me.wait()
            c8 = lambda i: at(85.625 + (5 * CH * 4 + 8 * i) / KB, CH)
            best, low = c8(1), c8(2)

            def first_best(x, top, hot, tmp):
                did(v.tensor_reduce(top, x, AXX, ALU.max))
                did(v.tensor_tensor(tmp, x, bj(top, 4), ALU.is_equal))
                did(v.tensor_tensor(tmp, tmp, iota4, ALU.mult))
                did(v.tensor_reduce(low, tmp, AXX, ALU.min))
                did(v.tensor_tensor(hot, bj(low, 4), iota4, ALU.is_equal))
            hotg, hot1, hot2, tmp4, sel = R1(1), R1(2), R1(3), R1(4), at(85.625 + (5 * CH * 4 + 64) / KB, CH, 4)
            first_best(lg[:, :, 0:4], best, hotg, tmp4)
            v.tensor_tensor(R1(0), lg[:, :, 0:4], bj(best, 4), ALU.subtract).then_inc(S3["ex_in"], 1)
            el = lg[:, :, 4:20].rearrange("p j (g e) -> p j g e", e=4)
            A1, A2, A3, rk, tt_, pj = (R3(i) for i in range(6))
            q4 = lambda x: x.rearrange("p j (g e) -> p j g e", e=4)
            gb = hotg.unsqueeze(3).to_broadcast([P, CH, 4, 4])
            for j in range(CH):
                me.did(v.tensor_tensor(q4(A1)[:, j], el[:, j], gb[:, j], ALU.mult))
            me.wait()
            for j in range(CH):
                me.did(v.tensor_reduce(sel[:, j], q4(A1)[:, j].rearrange("p g e -> p e g"), AXX, ALU.add))
            me.wait()
            m1_, m2_, e2_ = c8(3), c8(4), c8(0)
            first_best(sel, m1_, hot1, tmp4)
            did(v.scalar_tensor_tensor(sel, hot1, -1e30, sel, ALU.mult, ALU.add))
            first_best(sel, m2_, hot2, tmp4)
            v.tensor_tensor(e2_, m2_, m1_, ALU.subtract).then_inc(S3["ex_in"], 1)
            for hot, dst in ((hot1, A1), (hot2, A2)):
                for j in range(CH):
                    me.did(v.tensor_tensor(q4(dst)[:, j], gb[:, j], hot[:, j].unsqueeze(1).to_broadcast([P, 4, 4]), ALU.mult))
            me.wait()
            v.tensor_tensor(A3, A1, A2, ALU.add).then_inc(S3["mask_ready"], 1)
            dve.wait_ge(S3["ex_out"], 2)
            did(v.tensor_reduce(best, R1(0), AXX, ALU.add))
            did(v.tensor_scalar(low, e2_, 1.0, None, ALU.add))
            did(v.tensor_tensor(best, best, low, ALU.mult))
            did(v.reciprocal(wsel[:, 0], best))
            did(v.tensor_tensor(wsel[:, 1], wsel[:, 0], e2_, ALU.mult))
            dve.wait_ge(S3["rank_job"], 1)
            me.did(v.tensor_copy(tt_, banks[3][:, 0:P].rearrange("p (j e) -> p j e", e=16)))
            did(v.memset(pj[:, 0], 0.0))
            for j in range(1, CH):
                did(v.tensor_tensor(pj[:, j], pj[:, j - 1], tt_[:, j - 1], ALU.add))
            cnt, inc, off, nt, tinc, tst, base = (RW(i) for i in (1, 2, 3, 5, 6, 7, 8))
            onesw = RW(4)
            did(v.tensor_tensor(cnt, pj[:, CH - 1], tt_[:, CH - 1], ALU.add))
            did(v.tensor_tensor_scan(inc, onesw, cnt, 0.0, ALU.mult, ALU.add))
            did(v.tensor_tensor(off, inc, cnt, ALU.subtract))
            did(v.tensor_tensor(rk, banks[2][:, 0:P].rearrange("p (j e) -> p j e", e=16), pj, ALU.add))
            did(v.tensor_tensor(rk, rk, off.unsqueeze(1).to_broadcast([P, CH, 16]), ALU.add))
            for k, mk in enumerate((A1, A2)):
                did(v.tensor_tensor(mk, mk, rk, ALU.mult))
                did(v.tensor_reduce(c8(3 + k), mk, AXX, ALU.add))
            did(v.tensor_copy(slots[:, 0:8], c8(3)))
            v.tensor_copy(slots[:, 8:16], c8(4)).then_inc(S3["slots_ready"], 1)
            did(v.tensor_scalar(nt, cnt, 1.0 / TT, (TT / 2 - 0.5) / TT, ALU.mult, ALU.add))
            did(v.tensor_scalar(nt, nt, ROUND, None, ALU.add))
            did(v.tensor_scalar(nt, nt, -ROUND, 1.0, ALU.add, ALU.max))
            did(v.tensor_tensor_scan(tinc, onesw, nt, 0.0, ALU.mult, ALU.add))
            did(v.tensor_tensor(tst, tinc, nt, ALU.subtract))
            did(v.scalar_tensor_tensor(base, tst, -float(TT), off, ALU.mult, ALU.add))
            did(v.tensor_copy(meta[:, 0:16], tst[0:1]))
            me.did(v.tensor_copy(meta[:, 16:17], tinc[0:1, 15:16]))
            did(v.tensor_copy(meta[:, 17:33], tinc[0:1]))
            NR = MAXT + 2
            gidx = at(190, NR, parts=1)
            ind, ind2 = at(180, NR, 16, parts=1), at(184, NR, 16, parts=1)
            dve.wait_ge(dm_scat, 16 * 2 * CH)
            did(v.memset(gidx, 1.0))
            did(v.tensor_tensor_scan(gidx, gidx, gidx, -1.0, ALU.mult, ALU.add))
            gb_ = gidx.unsqueeze(2).to_broadcast([1, NR, 16])
            eb = lambda x: x[0:1].unsqueeze(1).to_broadcast([1, NR, 16])
            did(v.tensor_tensor(ind, gb_, eb(tst), ALU.is_ge))
            did(v.tensor_tensor(ind2, gb_, eb(tinc), ALU.is_lt))
            did(v.tensor_tensor(ind, ind, ind2, ALU.mult))
            did(v.tensor_tensor(ind, ind, eb(base), ALU.mult))
            rr_ = at(191, NR, parts=1)
            did(v.tensor_reduce(rr_, ind, AXX, ALU.add))
            did(v.scalar_tensor_tensor(rr_, gidx, float(TT), rr_, ALU.mult, ALU.add))
            did(v.tensor_scalar(rr_, rr_, float(PADROW), None, ALU.min))
            did(v.memset(yTs, 0.0))
            did(v.memset(rowtab[:, 0:1], TRASH))
            v.tensor_copy(rowtab[:, 1:1 + NR], rr_).then_inc(S3["route_end"], 1)

            dve.wait_ge(S3["route_end"], 1)
            with dve.Fori(0, NE) as e:
                a = dve.value_load(meta[:, bass.ds(e, 1)], min_val=0, max_val=MAXT)
                b = dve.value_load(meta[:, bass.ds(e + 1, 1)], min_val=1, max_val=MAXT)
                with dve.Fori(a, b) as n:
                    dve.wait_ge(S4["w2_job"], n)
                    for f in range(4):
                        dve.wait_ge(S4["sl_ready"], 4 * n + f + 1)
                        v.tensor_tensor(hT[:, f], sl[:, f], banks[f][:, TT:2 * TT], ALU.mult).then_inc(S4["hT_ready"], 1)
                    dve.wait_ge(S4["w2_job"], n + 1)
                    dve.wait_ge(S4["yt_job"], 2 * n + 2)
                    v.tensor_copy(yTs, banks[5][:].rearrange("p (k n) -> p k n", n=TT)).then_inc(S4["yt_copied"], 1)

            dve.wait_ge(dm_gf, 16)
            for j in range(CH):
                f_ = fin[j % 2]
                dve.wait_ge(dm_g1y[j % 2], 16 * (j // 2 + 1))
                if j >= 2:
                    dve.wait_ge(dm_out[j % 2], 16 * (j // 2))
                did(v.tensor_scalar(f_, y1[j % 2], wsel[:, 0, j:j + 1], None, ALU.mult))
                dve.wait_ge(dm_g2y[j % 2], 16 * (j // 2 + 1))
                v.scalar_tensor_tensor(f_, y2[j % 2], wsel[:, 1, j:j + 1], f_, ALU.mult, ALU.add).then_inc(S5["u2"], 1)
                dve.wait_ge(S5["u2"], j + 1)
                did(v.tensor_tensor(f_, f_, rows[:, 3], ALU.mult))
                v.tensor_tensor(f_, f_, x2[:, j], ALU.add).then_inc(S5["x3_ready"], 1)
                dve.wait_ge(S5["ss5_ready"], j + 1)
                v.tensor_scalar(ss5[:, j:j + 1], ss5[:, j:j + 1], 1.0 / D, EPS, ALU.mult, ALU.add).then_inc(S5["ms5_ready"], 1)
                dve.wait_ge(S5["sd5_ready"], j + 1)
                did(v.reciprocal(rstd5[:, j:j + 1], rstd5[:, j:j + 1]))
                v.scalar_tensor_tensor(f_, f_, rstd5[:, j:j + 1], gfrow, ALU.mult, ALU.mult).then_inc(S5["o_ready"], 1)

        @block.tensor
        def _(pe):
            for i, job, e, n in plan:
                if i >= 8:
                    _, _, e8, n8 = plan[i - 8]
                    pe.wait_ge(evac[e8], n8)
                bank = banks[i % 8]
                kind = job[0]
                if kind == "modcol":
                    pe.wait_ge(silubc_ready, 1)
                    for c in range(4):
                        pe.wait_ge(dm_wmod[c % 2], 16 * (c // 2 + 1))
                        for m in range(4):
                            for k in range(KD):
                                mm = nc.tensor.matmul(bank[:, 2 * (4 * c + m):2 * (4 * c + m) + 2],
                                                      wmod[c % 2][:, k, P * m:P * m + P], silu_c[:, k, :],
                                                      start=(k == 0), stop=(k == KD - 1))
                        if c < 3:
                            mm.then_inc(wmod_used, 1)
                        else:
                            mm.then_inc(pe_job, 1)
                    continue
                if kind == "xT":
                    _, grp, k = job
                    if k == 0:
                        pe.wait_ge(xs_ready, grp + 1)
                        if grp == 0:
                            pe.wait_ge(ident_ready, 1)
                            after_evac(pe, ("modcol",))
                    for s, i2 in enumerate(tiles_of(grp)):
                        v = xs[:, i2, P * k:P * k + P] if i2 < 8 else xc[:, i2 - 8, P * k:P * k + P]
                        mm = nc.tensor.transpose(bank[:, P * s:P * s + P], v, ident)
                elif kind == "u":
                    j = job[1]
                    if j == 0:
                        pe.wait_ge(dm_win[0], 16)
                        after_evac(pe, ("xT", 2, 6))
                        after_evac(pe, ("xT", 2, 7))
                    for k in range(KD):
                        mm = nc.tensor.matmul(bank[:], xT[:, k, P * j:P * j + P], w_u[:, k, :],
                                              start=(k == 0), stop=(k == KD - 1))
                elif kind == "U":
                    _, q, part = job
                    if q == 0 and part == "lat":
                        after_evac(pe, ("u", 8))
                        after_evac(pe, ("u", 9))
                    for g in range(QG):
                        if part == "lat":
                            mm = nc.tensor.transpose(bank[:, P * g:P * g + P], utok[:, QG * q + g].rearrange("p j h -> p (j h)"), ident)
                        else:
                            mm = nc.tensor.transpose(bank[:, NC_ * g:NC_ * g + NC_], utokc[0:NC_, QG * q + g].rearrange("p j h -> p (j h)"),
                                                     ident[0:NC_, 0:NC_])
                elif kind in "rq":
                    _, m, nn = job
                    w = w_r if kind == "r" else w_q
                    if m == 0 and nn == 0:
                        pe.wait_ge(dm_win[1 if kind == "r" else 2], 16)
                    n0, n1 = 512 * nn, min(512 * nn + 512, NTOK)
                    for k in range(KD):
                        mm = nc.tensor.matmul(bank[:, 0:n1 - n0], w[:, k, P * m:P * m + P], xT[:, k, n0:n1],
                                              start=(k == 0), stop=(k == KD - 1))
                elif kind == "modrow":
                    c = job[1] + 4
                    pe.wait_ge(dm_wmod[c % 2], 16 * (c // 2 + 1))
                    for k in range(KD):
                        mm = nc.tensor.matmul(bank[:], silu_bc[:, k, :], wmod[c % 2][:, k, :],
                                              start=(k == 0), stop=(k == KD - 1))
                mm.then_inc(pe_job, 1)

            pe.wait_ge(act_evac, count["act"])
            pe.wait_ge(dve_evac, count["dve"])
            with pe.Fori(0, 4) as i:
                for s_ in range(2):
                    q = 2 * i + s_
                    pe.wait_ge(S2["bt_ready"], q + 1)
                    for b in range(2):
                        pe.wait_ge(S2["s_taken"], 8 * q)
                        for g in range(4):
                            mm = nc.tensor.transpose(banks[3 + b][:, P * g:P * g + P], bt[:, 4 * b + g].rearrange("p j h -> p (j h)"), ident)
                        mm.then_inc(S2["btp_ready"], 1)
                    pe.wait_ge(S2["ct_ready"], q + 1)
                    if s_ == 0:
                        pe.wait_ge(S2["zT_ready"], 2 * i)
                    for b in range(2):
                        for g in range(2):
                            gg = 2 * b + g
                            o = banks[5 + b][0:GH, 240 * g:240 * g + 240]
                            nc.tensor.matmul(o[:, 112:240], bt[:, gg, 7], ct[:, gg, 0:8].rearrange("p j h -> p (j h)"), start=True, stop=False, skip_group_check=True)
                            mm = nc.tensor.matmul(o[:, 0:128], bt[:, 4 + gg, 0], ct[:, 4 + gg, 1:9].rearrange("p j h -> p (j h)"), start=False, stop=True, skip_group_check=True)
                    mm.then_inc(S2["taps_ready"], 1)
                    if s_ == 0:
                        pe.wait_ge(dm_wgm, 16 * (i + 1))
                        pe.wait_ge(S2["xc_ready"], i + 1)
                    for gi in range(6):
                        gate, ch = gi // 3, gi % 3
                        a, b = GCH[ch]
                        pe.wait_ge(S2["tri_ready"], 6 * q + gi - 2 if gi >= 2 else 6 * q)
                        nc.tensor.matmul(banks[gi % 3][:, 0:b - a], wgm[:, 2 * s_ + gate], xcv[:, a:b], start=True, stop=True).then_inc(S2["gate_ready"], 1)
                    pe.wait_ge(S2["uq_ready"], q + 1)
                    pe.wait_ge(S2["wk_ready"], q + 1)
                    pe.wait_ge(S2["btT_ready"], 2 * q + 2)
                    for pr in range(4):
                        for part in range(2):
                            if pr >= 2:
                                pe.wait_ge(S2["s_taken"], 8 * q + 2 * (pr - 2) + part + 1)
                            for g in range(2):
                                dg = 2 * pr + g
                                mm = nc.tensor.matmul(banks[3 + (2 * pr + part) % 4][:, NCH * g:NCH * g + NCH],
                                                      btT[:, dg, 64 * part:64 * part + P], uq[:, dg % 4], start=True, stop=True)
                            mm.then_inc(S2["s_ready"], 1)
                    pe.wait_ge(dm_toep, 128 * (q + 1))
                    pe.wait_ge(S2["pf_ready"], q + 1)
                    pe.wait_ge(S2["z_ready"], q)
                    for g in range(QG):
                        o = banks[7][:, P * g:P * g + P]
                        nc.tensor.matmul(o, uq[:, g, NC_:NCH], toep[:, g], start=True, stop=False)
                        for d in range(2):
                            k0 = 1 - d
                            dg = 4 * d + g
                            nc.tensor.matmul(o, p1[:, dg], ct[:, dg, k0:k0 + 8].rearrange("p j h -> p (j h)"), start=False, stop=False)
                            mm = nc.tensor.matmul(o, p2[:, dg], cs[:, dg, k0:k0 + 8].rearrange("p j h -> p (j h)"), start=False, stop=(d == 1))
                    mm.then_inc(S2["y_ready"], 1)
                pe.wait_ge(S2["z_ready"], 2 * i + 2)
                for b in range(2):
                    for j in range(4):
                        mm = nc.tensor.transpose(banks[5 + b][:, P * j:P * j + P], zq[:, 4 * b + j], ident)
                    mm.then_inc(S2["zp_ready"], 1)

            pe.wait_ge(S2["zT_ready"], 8)
            pe.wait_ge(S2["s_taken"], 8 * NQ)
            pe.wait_ge(S2["tri_ready"], 6 * NQ)
            pe.wait_ge(dm_wglu, 16)
            for n in range(8):
                m, h = n // 2, n % 2
                if n >= 2:
                    pe.wait_ge(S3["sig_ready"], n - 1)
                for k in range(4):
                    mm = nc.tensor.matmul(banks[n % 2][:], wglu[:, k, P * m:P * m + P], zT[:, k, 512 * h:512 * h + 512],
                                          start=(k == 0), stop=(k == 3))
                mm.then_inc(S3["glu_job"], 1)
            pe.wait_ge(dm_wout, 16)
            pe.wait_ge(S3["s5T_ready"], 8)
            pe.wait_ge(S2["hs_done"], 4)

            def router(j):
                pe.wait_ge(S3["h2_ready"], j + 1)
                if j:
                    pe.wait_ge(S3["h2T_ready"], 2 * j)
                for b in range(2):
                    for k in range(4):
                        c0 = P * (4 * b + k)
                        mm = nc.tensor.transpose(banks[6 + b][:, P * k:P * k + P], h2[:, j, c0:c0 + P], ident)
                    mm.then_inc(S3["h2T_job"], 1)

            def logit_mm(j):
                pe.wait_ge(S3["h2T_ready"], 2 * j + 2)
                if j == 0:
                    pe.wait_ge(dm_wr, 16)
                    pe.wait_ge(S3["sig_ready"], 8)
                if j >= 2:
                    pe.wait_ge(S3["lg_ready"], j - 1)
                for k in range(KD):
                    mm = nc.tensor.matmul(banks[j % 2][:, 0:20], h2T[j % 2][:, k], wr[:, k], start=(k == 0), stop=(k == KD - 1))
                mm.then_inc(S3["lg_job"], 1)

            for j in range(CH + 2):
                if j < CH:
                    for h in range(2):
                        if 2 * j + h >= 4:
                            pe.wait_ge(S3["mul_ready"], 2 * j + h - 3)
                        for k in range(KD):
                            lhs = s5T[:, k] if k < 4 else gq[:, k - 4]
                            mm = nc.tensor.matmul(banks[2 + (2 * j + h) % 4][:], lhs[:, P * j:P * j + P], wout[:, k, 512 * h:512 * h + 512],
                                                  start=(k == 0), stop=(k == KD - 1))
                        mm.then_inc(S3["out_job"], 1)
                if j >= 2:
                    router(j - 2)
                    logit_mm(j - 2)
            pe.wait_ge(S3["mask_ready"], 1)
            pe.wait_ge(S3["tri_built"], 1)
            pe.wait_ge(S3["mul_ready"], 16)
            mask = R3(2).rearrange("p j e -> p (j e)")
            nc.tensor.matmul(banks[2][:, 0:P], ltri, mask, start=True, stop=True)
            nc.tensor.matmul(banks[3][:, 0:P], ones, mask, start=True, stop=True).then_inc(S3["rank_job"], 1)

            def transpose_x():
                alone(pe)
                for k in range(KD):
                    mm = nc.tensor.transpose(banks[4][:, TT * k:TT * k + TT], xg[:, P * k:P * k + P], ident[0:TT, 0:TT])
                mm.then_inc(S4["xt_job"], 1)

            def transpose_y():
                alone(pe)
                for h in range(2):
                    for k in range(4):
                        mm = nc.tensor.transpose(banks[6 + h][0:TT, P * k:P * k + P], yTs[:, 4 * h + k], ident)
                    mm.then_inc(S4["yt_job"], 1)
            pe.wait_ge(S3["route_end"], 1)
            pe.wait_ge(dm_xg, 16)
            transpose_x()
            with pe.Fori(0, NE // 2) as ep:
                for s_ in range(2):
                    e = 2 * ep + s_
                    a = pe.value_load(meta[:, bass.ds(e, 1)], min_val=0, max_val=MAXT)
                    b = pe.value_load(meta[:, bass.ds(e + 1, 1)], min_val=1, max_val=MAXT)
                    pe.wait_ge(dm_w[s_], 48 * (ep + 1))
                    alone(pe)
                    with pe.Fori(a, b) as n:
                        pe.wait_ge(S4["xt_evac"], n + 1)
                        pe.wait_ge(S4["hT_ready"], 4 * n)
                        for f in range(4):
                            for w_, c0 in ((ew1[s_], 0), (ew3[s_], TT)):
                                for k in range(KD):
                                    mm = nc.tensor.matmul(banks[f][:, c0:c0 + TT], w_[:, k, P * f:P * f + P], xgT[:, k],
                                                          start=(k == 0), stop=(k == KD - 1))
                            mm.then_inc(S4["h_job"], 1)
                        pe.wait_ge(S4["yt_copied"], n)
                        pe.wait_ge(S4["y_evac"], 2 * n)
                        transpose_y()
                        pe.wait_ge(dm_xg, 16 * n + 32)
                        transpose_x()
                        for f in range(4):
                            pe.wait_ge(S4["hT_ready"], 4 * n + f + 1)
                            for k in range(KD):
                                mm = nc.tensor.matmul(banks[5][:, TT * k:TT * k + TT], ew2[s_][:, f, P * k:P * k + P], hT[:, f],
                                                      start=(f == 0 and k == 0), stop=(f == 3), skip_group_check=True)
                        mm.then_inc(S4["w2_job"], 1)
            last = pe.value_load(meta[:, NE:NE + 1], min_val=1, max_val=MAXT)
            pe.wait_ge(S4["yt_copied"], last)
            pe.wait_ge(S4["y_evac"], 2 * last)
            transpose_y()


def kernel(**inputs):
    import numpy as np
    import concourse.bacc as bacc
    from concourse import mybir as mb
    from concourse.bass_utils import run_bass_kernel_spmd

    a = {k: np.asarray(v) for k, v in inputs.items()}

    def col(v, n):
        return v.reshape(n, P).T

    def stack(v):
        return np.concatenate([v, v], 0)

    parts = {}
    parts["c"] = np.stack([col(a["c"][0], 8), col(a["c_ctx"], 8)], -1).reshape(P, 16)
    parts["bmod"] = col(a["b_mod"][0][:2 * D], 16)
    parts["g1"] = col(a["norm1_g"][0], 8)

    def states(v):
        return v.reshape(2, NQ, QG, ST).transpose(3, 1, 0, 2).reshape(ST, 64)
    parts["are"] = stack(states(a["s5_a_re"][0]))
    parts["aim"] = stack(states(a["s5_a_im"][0]))
    parts["ldt"] = np.broadcast_to(a["s5_log_dt"][0].reshape(2, NQ, QG).transpose(1, 0, 2).reshape(1, 64), (P, 64))
    dsk = np.zeros((P, 32), np.float32)
    dsk[:GH] = a["s5_d"][0].reshape(GRP, GH).T
    parts["dsk"] = dsk
    parts["bglu"] = col(a["s5_b_glu"][0], 4)
    parts["convw"] = a["lru_conv_w"][0].reshape(4, 4, P).transpose(2, 1, 0).reshape(P, 16)
    parts["convb"] = col(a["lru_conv_b"][0], 4)
    parts["bgate"] = np.stack([a["lru_b_a"][0], a["lru_b_x"][0]], 1).reshape(2, 2, 4, P).transpose(3, 0, 1, 2).reshape(P, 16)
    parts["lam"] = a["lru_lam"][0].reshape(2, 4, P).transpose(2, 0, 1).reshape(P, 8)
    parts["rbias"] = np.broadcast_to(np.concatenate([a["moe_b_group"][0], a["moe_b_router"][0].reshape(16)])[None], (P, 20))
    smalls = np.concatenate([parts[k] for k in SM], 1)

    def bmat(v):
        return v.reshape(2, NQ, QG, ST, GH).transpose(3, 1, 0, 2, 4).reshape(ST, 1024)

    def cmat(v):
        return v.reshape(2, NQ, QG, GH, ST).transpose(4, 1, 0, 2, 3).reshape(ST, 1024)
    br, bi, cr, ci = bmat(a["s5_b_re"][0]), bmat(a["s5_b_im"][0]), cmat(a["s5_c_re"][0]), cmat(a["s5_c_im"][0])
    bcs = np.concatenate([np.concatenate([br, bi]), np.concatenate([bi, br]),
                          np.concatenate([cr, ci]), np.concatenate([ci, cr])], 1)
    wg = np.zeros((P, 4, 2, 2, P), np.float32)
    for g, name in enumerate(("lru_w_a", "lru_w_x")):
        w = a[name][0]
        for h in range(8):
            s = 64 * (h % 2)
            wg[s:s + 64, h // 2, :, g, s:s + 64] = w[:, h].transpose(1, 0, 2)
    arrays = {
        "x": a["x"][0],
        "ctx": a["ctx"][0].reshape(NC_, CH, D).transpose(1, 0, 2).reshape(2, P, D),
        "smalls": smalls, "bc": bcs, "wg": wg.reshape(P, 2048),
        "w_mod": a["w_mod"][0], "b_mod": a["b_mod"][0], "w_in": a["w_in"][0], "w_out": a["w_out"][0],
        "w_glu": a["s5_w_glu"][0], "g2": a["norm2_g"][0], "gf": a["final_g"],
        "w_router": np.concatenate([a["moe_w_group"][0], a["moe_w_router"][0].transpose(1, 0, 2).reshape(D, 16)], 1),
        "w1": a["moe_w1"][0], "w3": a["moe_w3"][0], "w2": a["moe_w2"][0],
    }
    nc = bacc.Bacc("TRN2", target_bir_lowering=False, num_devices=1)
    t = {}
    for name, v in arrays.items():
        arrays[name] = v = np.ascontiguousarray(v)
        t[name] = nc.dram_tensor(name, v.shape, mb.dt.from_np(v.dtype), kind="ExternalInput").ap()
    out = nc.dram_tensor("out", (SEQ, D), mb.dt.float32, kind="ExternalOutput").ap()
    program(nc, t, out)
    r = run_bass_kernel_spmd(nc, [arrays], core_ids=[0])
    return np.asarray(r.results[0]["out"]).reshape(1, SEQ, D)
```

```python
import math
from contextlib import ExitStack

import concourse.bass as bass
from concourse import mybir
from concourse.alu_op_type import AluOpType as ALU

ACT = mybir.ActivationFunctionType
AXX = mybir.AxisListType.X
F32 = mybir.dt.float32
I32 = mybir.dt.int32
U32 = mybir.dt.uint32

P = 128
D = 1024
KD = D // P
SEQ, CTX = 1024, 256
CH = 8
NL, NC_ = SEQ // CH, CTX // CH
NCH = NL + NC_
NTOK = SEQ + CTX
DS5, DLRU = 512, 512
GRP, GH, ST = 32, 16, 64
NQ, QG = 8, 4
EPS = 1e-6
NE, FE = 16, 512
ROWS, COLS = 16, 64
KB = 256

SM = {}
_at = 0
for _name, _w in (("c", 16), ("bmod", 16), ("g1", 8), ("are", 64), ("aim", 64), ("ldt", 64),
                  ("dsk", 32), ("bglu", 4), ("convw", 16), ("convb", 4), ("bgate", 16), ("lam", 8),
                  ("rbias", 20)):
    SM[_name] = (_at, _at + _w)
    _at += _w
NSM = _at


class Tally:

    def __init__(self, eng, sem):
        self.eng, self.sem, self.n = eng, sem, 0

    def did(self, ins):
        ins.then_inc(self.sem, 1)
        self.n += 1
        return self.n

    def wait(self):
        self.eng.wait_ge(self.sem, self.n)


def program(nc, t, out):
    with ExitStack() as ctx:
        def sem(name):
            return ctx.enter_context(nc.semaphore(name))

        arena = ctx.enter_context(nc.sbuf_tensor("arena", [P, 204 * KB], F32))
        sm = ctx.enter_context(nc.sbuf_tensor("small", [P, 984], F32))
        banks = [ctx.enter_context(nc.psum_tensor(f"bank{i}", [P, 512], F32)) for i in range(8)]

        def at(kb, *dims, parts=P):
            n = math.prod(dims)
            o = int(kb * KB)
            v = arena[0:parts, o:o + n]
            if len(dims) == 2:
                v = v.rearrange("p (a b) -> p a b", b=dims[1])
            if len(dims) == 3:
                v = v.rearrange("p (a b c) -> p a b c", b=dims[1], c=dims[2])
            if len(dims) == 4:
                v = v.rearrange("p (a b c d) -> p a b c d", b=dims[1], c=dims[2], d=dims[3])
            return v

        def small(name):
            return sm[:, SM[name][0]:SM[name][1]]

        xT = at(0, KD, NTOK)
        w_u, w_r, w_q = (at(40 + 16 * i, KD, 512) for i in range(3))
        wmod = [at(88 + 16 * i, KD, 512) for i in range(2)]
        xs = at(120, 8, D)
        xc = at(168, 2, D)
        junk = at(176, D)
        silu_bc = at(188, KD, P)
        mrow = at(192, 2 * D, parts=2)
        utok = at(120, GRP, CH, GH)
        utokc = at(136, GRP, CH, GH)
        U = at(168, GRP, NCH)
        rows = at(152, 4, D)
        RPAD = 2 + CTX + 1 + 2 + SEQ + 1
        rS = at(120, 4, RPAD)
        gq = at(40, 4, SEQ)
        LAT0 = 2 + CTX + 1 + 2

        RL = RPAD - 3
        CL0 = CTX + 3
        zT = at(0, 4, SEQ)
        cosn, sinn = at(16, 8, NCH), at(21, 8, NCH)
        t1, t2 = at(26, 8, NCH), at(31, 8, NCH)
        uq = at(36, QG, NCH)
        bt = at(56, 8, CH, GH)
        ct, cs = at(60, 8, CH + 1, GH), at(64.5, 8, CH + 1, GH)
        ctmp = at(69, 8, CH + 1, GH)
        cstmp = at(117.5, 4, CH + 1, GH)
        btT = at(73.5, 8, 192)
        wk = at(79.5, QG, 240, parts=GH)
        toep = at(83.25, QG, P)
        tr, ti = at(88, RL), at(93.0625, RL)
        la, sq = at(98.125, RL), at(103.1875, RL)
        xcv = at(108.25, RL)
        hf = at(113.5, SEQ)
        gh = at(140.25, 8, NCH)
        ctmp_d = at(149.5, QG, GH, parts=GH)
        zq = at(145.5, CH, P)
        p1, p2 = at(26, 8, NL), at(31, 8, NL)
        bcq = [at(188 + 2 * i, 4, P) for i in range(2)]
        wgm = at(201, 4, P)
        pwr, pwi = at(192, 64, 17), at(196.25, 64, 17)
        ph, phc, mag = at(152, 64, 17), at(156.25, 64, 17), at(160.5, 64, 17)
        pt = [at(164.75 + 0.25 * i, 64) for i in range(12)]

        s5T = at(16, 4, SEQ)
        wglu = at(32, 4, DS5)
        wout = at(88, KD, D)
        x2 = at(120, CH, D)
        h2 = at(168, CH, D)
        xt = [at(56 + 4 * i, D) for i in range(2)]
        h2T = [at(64 + 4 * i, KD, P) for i in range(2)]
        wr = at(72, KD, 20)
        g2row = at(76, D)
        junk3 = at(80, D)
        ltri, ones = at(84, P), at(84.5, P)
        lg = at(85, CH, 20)
        R1 = lambda i: at(85.625 + i * CH * 4 / KB, CH, 4)
        R3 = lambda i: at(73 + i * 0.5, CH, 16)
        RW = lambda i: at(86.75 + i * 16 / KB, 16)

        TT = 128
        MAXT = 2 * SEQ // TT + NE
        PADROW = 2 * SEQ
        ew1 = [at(48 * i, KD, FE) for i in range(2)]
        ew3 = [at(48 * i + 16, KD, FE) for i in range(2)]
        ew2 = [at(48 * i + 32, 4, D) for i in range(2)]
        xgT, sl, hid, hT = at(96, KD, TT), at(100, FE), at(102, FE), at(104, 4, TT)
        xg, ysb = at(172, D), at(176, D)
        NB5 = 4
        y1, y2, fin = ([at(16 * a + 4 * i, D) for i in range(NB5)] for a in range(3))
        gfrow, junk5 = at(192, D), at(196, D)
        xs_dram = nc.dram_tensor("tokens_by_expert", [2 * SEQ + TT, D], F32).ap()
        ys_dram = nc.dram_tensor("outputs_by_expert", [2 * SEQ + TT, D], F32).ap()

        o = NSM
        silu_c = sm[:, o:o + 16].rearrange("p (k v) -> p k v", v=2); o += 16
        shcol = sm[:, o:o + 16].rearrange("p (k v) -> p k v", v=2); o += 16
        sccol = sm[:, o:o + 16].rearrange("p (k v) -> p k v", v=2); o += 16
        ss = sm[:, o:o + 10]; o += 10
        rstd = sm[:, o:o + 10]; o += 10
        ident = sm[:, o:o + P]; o += P

        fi = sm[:, o:o + 64]; o += 64
        r8 = sm[:, o:o + 64]; o += 64
        n8 = sm[:, o:o + NCH]; o += NCH
        kx = sm[:, o:o + 34].rearrange("p (d k) -> p d k", k=17); o += 34
        n8i, kxi, fii = n8.bitcast(I32), kx.bitcast(I32), fi.bitcast(I32)
        sgn = sm[:, o:o + 2]; o += 2
        quarter = sm[:, o:o + 1].bitcast(I32); o += 1
        halfl, nhalfl = sm[:, o:o + 8], sm[:, o + 8:o + 16]; o += 16
        hbg = sm[:, o:o + 16]; o += 16
        assert o <= 984, o
        wsel = sm[:, 0:16].rearrange("p (k j) -> p k j", j=CH)
        slots = sm[:, 16:32].bitcast(U32)
        meta = sm[0:1, 32:32 + 64].bitcast(I32)
        rowtab = sm[0:1, 96:96 + MAXT + 3].bitcast(I32)
        ss3, rstd3 = sm[:, 160:168], sm[:, 168:176]
        ss5, rstd5 = sm[:, 176:184], sm[:, 184:192]
        TURN = 2.0 * math.pi * (1 - 2.0 ** -23) / 2.0 ** 32

        dm_small, dm_bc, dm_rowb = sem("dm_small"), sem("dm_bc"), sem("dm_rowb")
        dm_wmod = [sem(f"dm_wmod{i}") for i in range(2)]
        dm_x = [sem(f"dm_x{i}") for i in range(3)]
        dm_win = [sem(f"dm_win{i}") for i in range(3)]
        ident_ready = sem("ident_ready")
        silu_ready, silubc_ready = sem("silu_ready"), sem("silubc_ready")
        mrow_job, mrow_ready = sem("mrow_job"), sem("mrow_ready")
        ss_ready, ms_ready, sd_ready, xs_ready = sem("ss_ready"), sem("ms_ready"), sem("sd_ready"), sem("xs_ready")
        pe_job, act_evac, dve_evac = sem("pe_job"), sem("act_evac"), sem("dve_evac")
        act_self, dve_self, pool_self = sem("act_self"), sem("dve_self"), sem("pool_self")
        pads_ready = sem("pads_ready")
        ints_ready, fi_ready, ph_ready, trig_ready, mag_in, dt_ready = (sem(n) for n in (
            "ints_ready", "fi_ready", "ph_ready", "trig_ready", "mag_in", "dt_ready"))
        sgn_ready = sem("sgn_ready")
        prep_done, sp_in, sp_exp = sem("prep_done"), sem("sp_in"), sem("sp_exp")

        jobs = [("modcol",)]
        for grp in range(3):
            jobs += [("xT", grp, k) for k in range(KD)]
        jobs += [("u", j) for j in range(10)]
        jobs += [("U", q, part) for q in range(NQ) for part in ("lat", "ctx")]
        rq = [("r", m, n) for m in range(4) for n in range(3)] + [("q", m, n) for m in range(4) for n in range(2)]
        mr = [("modrow", i) for i in range(8)]
        for i, job in enumerate(rq):
            jobs.append(job)
            if i % 2 == 1 and mr:
                jobs.append(mr.pop(0))
        jobs += mr

        def drainer(i, job):
            if job[0] in ("q",):
                return "act"
            if job[0] in ("modcol", "modrow"):
                return "dve"
            return ("act", "dve")[i % 2]

        plan, count = [], {"act": 0, "dve": 0}
        for i, job in enumerate(jobs):
            e = drainer(i, job)
            count[e] += 1
            plan.append((i, job, e, count[e]))
        evac = {"act": act_evac, "dve": dve_evac}
        place = {job: (i, e, n) for i, job, e, n in plan}

        def after_evac(eng, job):
            _, e, n = place[job]
            eng.wait_ge(evac[e], n)

        def tiles_of(grp):
            return (range(0, 4), range(4, 8), range(8, 10))[grp]

        def evacuate(eng, e, i, job, n):
            bank = banks[i % 8]
            done = evac[e]

            def copy(dst, src):
                if e == "act":
                    return nc.scalar.activation(dst, src, ACT.Copy)
                return nc.vector.tensor_copy(dst, src)

            kind = job[0]
            if kind == "xT":
                _, grp, k = job
                v = int(grp == 2)
                w = P * len(tiles_of(grp))
                dst = xT[:, k, 512 * grp:512 * grp + w]
                if e == "act":
                    ins = nc.scalar.activation(dst, bank[:, 0:w], ACT.Identity, bias=shcol[:, k, v:v + 1],
                                               scale=sccol[:, k, v:v + 1])
                else:
                    ins = nc.vector.tensor_scalar(dst, bank[:, 0:w], sccol[:, k, v:v + 1], shcol[:, k, v:v + 1],
                                                  ALU.mult, ALU.add)
            elif kind == "u":
                j = job[1]
                if j < 8:
                    ins = copy(utok[:, :, j], bank[:].rearrange("p (g h) -> p g h", h=GH))
                else:
                    for jq in range(4):
                        ins = copy(utokc[0:NC_, :, 4 * (j - 8) + jq],
                                   bank[32 * jq:32 * jq + 32, :].rearrange("p (g h) -> p g h", h=GH))
            elif kind == "U":
                _, q, part = job
                if part == "lat":
                    ins = copy(U[:, QG * q:QG * q + QG, NC_:NCH], bank[:].rearrange("p (g c) -> p g c", g=QG))
                else:
                    ins = copy(U[:, QG * q:QG * q + QG, 0:NC_], bank[:, 0:QG * NC_].rearrange("p (g c) -> p g c", g=QG))
            elif kind == "r":
                _, m, nn = job
                if nn == 2:
                    dst = rS[:, m, 2:2 + CTX].rearrange("p (c j) -> p j c", j=CH)
                    ins = copy(dst, bank[:, 0:CTX].rearrange("p (j c) -> p j c", j=CH))
                else:
                    v = rS[:, m, LAT0:LAT0 + SEQ].rearrange("p (cc j row) -> p j row cc", cc=8, j=8)[:, 4 * nn:4 * nn + 4]
                    src = bank[:].rearrange("p (j row cc) -> p j row cc", j=4, row=ROWS)
                    ins = copy(v, src)
            elif kind == "q":
                _, m, nn = job
                ins = nc.scalar.activation(gq[:, m, 512 * nn:512 * nn + 512], bank[:], ACT.Gelu_apprx_tanh)
            elif kind == "modrow":
                r = job[1]
                v = rows[:, r // 2, 512 * (r % 2):512 * (r % 2) + 512]
                if r == 0:
                    eng.wait_ge(dm_rowb, 16)
                ins = nc.vector.tensor_tensor(v, bank[:], v, ALU.add)
            ins.then_inc(done, 1)

        names2 = ("bt_ready", "ct_ready", "phase_ready", "turn_ready", "btp_ready", "btT_ready", "taps_ready",
                  "wk_ready", "uq_ready", "s_ready", "s_taken", "pf_ready", "y_ready",
                  "z_ready", "zp_ready", "zT_ready",                   "xc_ready", "gate_ready", "gate_taken", "tri_ready", "decay_ready", "sqin_ready", "root_ready",
                  "b_ready", "a2_ready", "h_ready", "hs_done", "part_y", "bc_ready", "cs_ready")
        S2 = {n: sem(n) for n in names2}
        dm_bcq = [sem(f"dm_bcq{i}") for i in range(2)]
        dm_wgm, dm_toep = sem("dm_wgm"), sem("dm_toep")
        scan_ctx, scan_lat = sem("scan_ctx"), sem("scan_lat")
        dve2, pool2, act2 = sem("dve2"), sem("pool2"), sem("act2")
        NJ = len(jobs)
        GCH = ((0, 512), (512, 1024), (1024, RL))

        names3 = ("glu_job", "sig_ready", "s5T_ready", "out_job", "mul_ready", "x2_ready", "ss3_ready", "ms3_ready",
                  "sd3_ready", "hn_ready", "h2_ready", "h2T_job", "h2T_ready", "lg_job", "lg_ready",                   "tri_built", "ex_in", "ex_out", "mask_ready", "rank_job", "slots_ready", "route_end", "zero_ready")
        S3 = {n: sem(n) for n in names3}
        dm_wglu, dm_wout, dm_wr, dm_g2 = sem("dm_wglu"), sem("dm_wout"), sem("dm_wr"), sem("dm_g2")
        dm_xt = [sem(f"dm_xt{i}") for i in range(2)]
        dm_scat = sem("dm_scat")
        names4 = ("h1_job", "h3_job", "sl_ready", "hid_ready", "ht_job", "hT_ready", "y_job", "y_evac", "xt_job", "xt_evac")
        S4 = {n: sem(n) for n in names4}
        dm_w = [sem(f"dm_w{i}") for i in range(2)]
        dm_xg, dm_y, dm_gf = sem("dm_xg"), sem("dm_y"), sem("dm_gf")
        dm_g1y, dm_g2y = [sem(f"dm_g1y{i}") for i in range(NB5)], [sem(f"dm_g2y{i}") for i in range(NB5)]
        names5 = ("u1", "u2", "x3_ready", "ss5_ready", "ms5_ready", "sd5_ready", "o_ready")
        S5 = {n: sem(n) for n in names5}
        dm_out = [sem(f"dm_out{i}") for i in range(NB5)]

        class Steps:

            def __init__(self, eng, sem_, i, per, apart=False):
                self.apart = apart
                self.eng, self.sem, self.base, self.n, self.per = eng, sem_, i * per, 0, per

            def did(self, ins):
                ins.then_inc(self.sem, 1)
                self.n += 1

            def wait(self):
                self.eng.wait_ge(self.sem, self.base + self.n)
                if self.apart:
                    alone(self.eng)

            def end(self):
                assert self.n == self.per, self.n

        def alone(eng):
            eng.sem_inc(waits_passed[eng.engine], 1)

        def rev(ap_of, a, b):
            return ap_of[:, b - 1:(a - 1 if a else None):-1]

        def hn_sum(pool, j):
            pool.wait_ge(S3["hn_ready"], j + 1)
            nc.gpsimd.tensor_tensor(h2[:, j], h2[:, j], rows[:, 1], ALU.add).then_inc(S3["h2_ready"], 1)

        dve3 = sem("dve3")
        waits_passed = {eng.engine: sem(f"waits_passed{i}") for i, eng in enumerate((nc.sync, nc.gpsimd, nc.scalar, nc.tensor, nc.vector))}
        block = ctx.enter_context(nc.Block())

        @block.sync
        def _(sp):
            wm = t["w_mod"].rearrange("(k p) n -> p k n", p=P)
            win = t["w_in"].rearrange("(k p) n -> p k n", p=P)

            def load_wmod(c):
                if 2 <= c <= 4:
                    sp.wait_ge(mrow_job, c - 1)
                elif c == 5:
                    sp.wait_ge(pe_job, 1)
                elif c > 5:
                    sp.wait_ge(pe_job, place[("modrow", c - 6)][0] + 1)
                sp.dma_start(wmod[c % 2], wm[:, :, 512 * c:512 * c + 512]).then_inc(dm_wmod[c % 2], 16)

            sp.dma_start(sm[:, 0:NSM], t["smalls"]).then_inc(dm_small, 16)
            load_wmod(0)
            load_wmod(1)
            xv = t["x"].rearrange("(c j) d -> c j d", j=CH)
            sp.dma_start(xs[:, 0:4], xv[:, 0:4]).then_inc(dm_x[0], 16)
            load_wmod(2)
            sp.dma_start(xs[:, 4:8], xv[:, 4:8]).then_inc(dm_x[1], 16)
            load_wmod(3)
            sp.dma_start(xc, t["ctx"].rearrange("t p d -> p t d")).then_inc(dm_x[2], 16)
            for i, w in enumerate((w_u, w_r, w_q)):
                sp.dma_start(w, win[:, :, 512 * i:512 * i + 512]).then_inc(dm_win[i], 16)
            sp.wait_ge(prep_done, 1)
            sp.dma_start(rows, t["b_mod"][2 * D:6 * D].rearrange("(a n) -> a n", n=D).partition_broadcast(P)).then_inc(dm_rowb, 16)
            for c in range(4, 12):
                load_wmod(c)

            sp.wait_ge(pe_job, NJ)
            sp.sem_inc(dm_toep, 1)
            bcv = t["bc"].rearrange("p (a q n) -> p a q n", a=4, q=NQ)
            wgv = t["wg"].rearrange("p (m b n) -> p m b n", m=4, b=4)

            def load_bc(q, s_):
                sp.dma_start(bcq[s_], bcv[:, :, bass.ds(q, 1), :].rearrange("p a q n -> p a (q n)")).then_inc(dm_bcq[s_], 16)

            def load_wg(m):
                sp.dma_start(wgm, wgv[:, bass.ds(m, 1)].rearrange("p m b n -> p (m b) n")).then_inc(dm_wgm, 16)

            def two_quads(i, more):
                for s_ in range(2):
                    q = 2 * i + s_
                    sp.wait_ge(S2["wk_ready"], q + 1)
                    sp.wait_ge(S2["y_ready"], 1 + q)
                    for ji in range(CH):
                        sp.dma_start(toep[GH * ji:GH * ji + GH], wk[:, :, GH * (7 - ji):GH * (7 - ji) + P]).then_inc(dm_toep, 16)
                    if more:
                        sp.wait_ge(S2["ct_ready"], 1 + q + 1)
                        sp.wait_ge(S2["cs_ready"], 1 + q + 1)
                        load_bc(q + 2, s_)
                if more:
                    sp.wait_ge(S2["gate_ready"], 1 + 12 * i + 12)
                    load_wg(i + 1)
            load_bc(0, 0)
            load_bc(1, 1)
            load_wg(0)
            with sp.Fori(0, 3) as i:
                two_quads(i, True)
            two_quads(3, False)

            sp.wait_ge(S2["hs_done"], 5)
            sp.wait_ge(S2["zT_ready"], 9)
            sp.dma_start(wglu, t["w_glu"].rearrange("(k p) n -> p k n", p=P)).then_inc(dm_wglu, 16)
            for j in range(2):
                sp.dma_start(xt[j], xv[:, j]).then_inc(dm_xt[j], 16)
            sp.dma_start(g2row, t["g2"].partition_broadcast(P)).then_inc(dm_g2, 16)
            sp.dma_start(wr, t["w_router"].rearrange("(k p) n -> p k n", p=P)).then_inc(dm_wr, 16)
            sp.dma_start(wout, t["w_out"].rearrange("(k p) n -> p k n", p=P)).then_inc(dm_wout, 16)
            w1v = t["w1"].rearrange("e (k p) f -> p e k f", p=P)
            w3v = t["w3"].rearrange("e (k p) f -> p e k f", p=P)
            w2v = t["w2"].rearrange("e (k p) d -> p e k d", p=P)
            sp.wait_ge(S3["s5T_ready"], 8)
            sp.dma_start(ew1[0], w1v[:, 0]).then_inc(dm_w[0], 16)
            for j in range(2, CH):
                sp.wait_ge(S3["x2_ready"], j - 1)
                sp.dma_start(xt[j % 2], xv[:, j]).then_inc(dm_xt[j % 2], 16)

            sp.wait_ge(S3["out_job"], 2 * CH)
            sp.dma_start(ew3[0], w3v[:, 0]).then_inc(dm_w[0], 16)
            sp.dma_start(ew2[0], w2v[:, 0]).then_inc(dm_w[0], 16)

            def load_expert(e, s_):
                one = lambda v: v[:, bass.ds(e, 1)].rearrange("p e k f -> p (e k) f")
                sp.dma_start(ew1[s_], one(w1v)).then_inc(dm_w[s_], 16)
                sp.dma_start(ew3[s_], one(w3v)).then_inc(dm_w[s_], 16)
                sp.dma_start(ew2[s_], one(w2v)).then_inc(dm_w[s_], 16)
            sp.wait_ge(S3["route_end"], 1)
            sp.wait_ge(dm_xg, 16)
            load_expert(1, 1)
            with sp.Fori(1, NE // 2) as ep:
                for s_ in range(2):
                    free = sp.value_load(meta[:, bass.ds(2 * ep + s_ + 15, 1)], min_val=0, max_val=MAXT)
                    sp.wait_ge(S4["y_job"], 2 * free)
                    load_expert(2 * ep + s_, s_)

            ov = out.rearrange("(c j) d -> c j d", j=CH)
            sp.dma_start(gfrow, t["gf"].partition_broadcast(P)).then_inc(dm_gf, 16)
            for j in range(CH):
                sp.wait_ge(S5["o_ready"], j + 1)
                sp.dma_start(ov[:, j], fin[j % NB5]).then_inc(dm_out[j % NB5], 16)
            for i in range(NB5):
                sp.wait_ge(dm_out[i], 16 * (CH // NB5))

        @block.gpsimd
        def _(pool):
            pool.memset(ident, 0.0).then_inc(pool_self, 1)
            pool.wait_ge(pool_self, 1)
            pool.affine_select(out=ident, in_=ident, compare_op=ALU.not_equal, fill=1.0, base=0,
                               pattern=[[-1, P]], channel_multiplier=1).then_inc(ident_ready, 1)
            for d, (a, b, base, step) in ((0, (0, 9, 0, 1)), (0, (9, 17, 7, -1)), (1, (0, 9, 8, -1)), (1, (9, 17, 0, 1))):
                pool.iota(kxi[:, d, a:b], [[step, b - a]], base=base, channel_multiplier=0).then_inc(ints_ready, 1)
            pool.iota(n8i, [[CH, NCH]], base=0, channel_multiplier=0).then_inc(ints_ready, 1)
            pool.iota(quarter, [[0, 1]], base=1 << 30, channel_multiplier=0).then_inc(ints_ready, 1)
            pool.wait_ge(ints_ready, 6)
            pool.wait_ge(fi_ready, 1)
            phi, phci = ph.bitcast(I32), phc.bitcast(I32)
            for d in range(2):
                dst = phi.rearrange("p (q d g) k -> p q d g k", d=2, g=QG)[:, :, d]
                f = fii.rearrange("p (q d g) -> p q d g", d=2, g=QG)[:, :, d]
                for q in range(NQ):
                    nc.gpsimd.tensor_tensor(dst[:, q], f[:, q].unsqueeze(2).to_broadcast([P, QG, 17]),
                                            kxi[:, d].unsqueeze(1).to_broadcast([P, QG, 17]), ALU.mult).then_inc(pool_self, 1)
            pool.wait_ge(pool_self, 17)
            nc.gpsimd.tensor_tensor(phci, phi, quarter.unsqueeze(2).to_broadcast([P, 64, 17]), ALU.add).then_inc(ph_ready, 1)

            pool.wait_ge(pe_job, NJ)
            pool.wait_ge(prep_done, 1)
            g = nc.gpsimd
            for n in ("ct_ready",):
                pool.sem_inc(S2[n], 1)
            shp = [P, 8, CH, GH]
            with pool.Fori(0, 4) as i:
                me = Steps(pool, pool2, i, 20, apart=True)

                def did(ins):
                    me.did(ins)
                    me.wait()

                for s_ in range(2):
                    q = 2 * i + s_
                    pool.wait_ge(dm_bcq[s_], 16 * (i + 1))
                    alone(pool)
                    X, Y = bcq[s_][:, 0].rearrange("p (a h) -> p a h", h=GH), bcq[s_][:, 1].rearrange("p (a h) -> p a h", h=GH)
                    CX, CY = bcq[s_][:, 2].rearrange("p (a h) -> p a h", h=GH), bcq[s_][:, 3].rearrange("p (a h) -> p a h", h=GH)
                    me.did(g.tensor_scalar(bcq[s_][:, 1], bcq[s_][:, 1], sgn[:, 0:1], None, ALU.mult))
                    me.did(g.tensor_scalar(bcq[s_][:, 2], bcq[s_][:, 2], sgn[:, 1:2], None, ALU.mult))
                    did(g.tensor_scalar(bcq[s_][:, 3], bcq[s_][:, 3], -1.0, None, ALU.mult))
                    g.nop().then_inc(S2["bc_ready"], 1)

                    def power(tab, a, n):
                        v = tab[:, bass.ds(8 * q, 8), a:a + n]
                        return v.unsqueeze(3).to_broadcast([P, 8, n, GH])

                    def over(x, n):
                        return x.unsqueeze(2).to_broadcast([P, 8, n, GH])
                    pool.wait_ge(S2["taps_ready"], 1 + q)
                    alone(pool)
                    me.did(g.tensor_tensor(bt, power(pwr, 9, 8), over(X, 8), ALU.mult))
                    did(g.tensor_tensor(ctmp[:, :, 0:8], power(pwi, 9, 8), over(Y, 8), ALU.mult))
                    did(g.tensor_tensor(bt, bt, ctmp[:, :, 0:8], ALU.add))
                    g.nop().then_inc(S2["bt_ready"], 1)
                    pool.wait_ge(S2["pf_ready"], 1 + q)
                    alone(pool)
                    ci, si = cosn.bitcast(I32), sinn.bitcast(I32)
                    f = fii[:, bass.ds(8 * q, 8)].unsqueeze(2).to_broadcast([P, 8, NCH])
                    did(g.tensor_tensor(si, f, n8i.unsqueeze(1).to_broadcast([P, 8, NCH]), ALU.mult))
                    g.tensor_tensor(ci, si, quarter.unsqueeze(2).to_broadcast([P, 8, NCH]), ALU.add).then_inc(S2["phase_ready"], 1)
                    pool.wait_ge(S2["y_ready"], 1 + q)
                    alone(pool)
                    me.did(g.tensor_tensor(ct, power(pwr, 0, 9), over(CX, 9), ALU.mult))
                    did(g.tensor_tensor(ctmp, power(pwi, 0, 9), over(CY, 9), ALU.mult))
                    did(g.tensor_tensor(ct, ct, ctmp, ALU.add))
                    g.nop().then_inc(S2["ct_ready"], 1)
                me.end()

            pool.wait_ge(S2["hs_done"], 5)
            pool.wait_ge(S2["zT_ready"], 9)
            g.memset(junk3, 0.0).then_inc(S3["zero_ready"], 1)
            pool.wait_ge(S3["zero_ready"], 1)
            g.dma_start(xs_dram[PADROW:PADROW + TT, :], junk3[0:TT]).then_inc(dm_y, 16)
            g.memset(ones, 1.0).then_inc(pool_self, 1)
            pool.wait_ge(pool_self, 18)
            g.affine_select(out=ltri, in_=ones, compare_op=ALU.is_gt, fill=0.0, base=0,
                            pattern=[[1, P]], channel_multiplier=-1).then_inc(S3["tri_built"], 1)
            for j in range(CH):
                pool.wait_ge(S3["mul_ready"], 2 * j + 2)
                pool.wait_ge(dm_xt[j % 2], 16 * (j // 2 + 1))
                g.tensor_tensor(x2[:, j], x2[:, j], xt[j % 2], ALU.add).then_inc(S3["x2_ready"], 1)
                if j:
                    hn_sum(pool, j - 1)
            hn_sum(pool, CH - 1)
            pool.wait_ge(S3["slots_ready"], 1)
            pool.wait_ge(S3["h2_ready"], CH)
            for k in range(2):
                for j in range(CH):
                    c0 = CH * k + j
                    g.indirect_dma_start(xs_dram[0:2 * SEQ, :], bass.IndirectOffsetOnAxis(ap=slots[:, c0:c0 + 1], axis=0),
                                         h2[:, j], None).then_inc(dm_scat, 16)
            pool.wait_ge(dm_scat, 16 * 2 * CH)
            pool.wait_ge(S3["route_end"], 1)
            g.dma_start(xg, xs_dram[0:TT, :]).then_inc(dm_xg, 16)
            row = pool.value_load(rowtab[:, 2:3], min_val=0, max_val=PADROW)
            pool.wait_ge(S4["xt_job"], 1)
            g.dma_start(xg, xs_dram[bass.ds(row, TT), :]).then_inc(dm_xg, 16)
            with pool.Fori(0, NE) as e:
                a = pool.value_load(meta[:, bass.ds(e, 1)], min_val=0, max_val=MAXT)
                b = pool.value_load(meta[:, bass.ds(e + 1, 1)], min_val=1, max_val=MAXT)
                with pool.Fori(a, b) as n:
                    row = pool.value_load(rowtab[:, bass.ds(n + 3, 1)], min_val=0, max_val=PADROW)
                    pool.wait_ge(S4["xt_job"], n + 2)
                    alone(pool)
                    g.dma_start(xg, xs_dram[bass.ds(row, TT), :]).then_inc(dm_xg, 16)
                    orow = pool.value_load(rowtab[:, bass.ds(n + 1, 1)], min_val=0, max_val=PADROW)
                    pool.wait_ge(S4["y_evac"], 1 + 2 * n + 2)
                    pool.wait_ge(dm_y, 16 * n + 16)
                    alone(pool)
                    g.dma_start(ys_dram[bass.ds(orow, TT), :], ysb).then_inc(dm_y, 16)
            last = pool.value_load(meta[:, NE:NE + 1], min_val=1, max_val=MAXT)
            pool.wait_ge(dm_y, 16 * last + 16)
            pool.wait_ge(dm_xg, 16 * last + 32)
            pool.wait_ge(S4["xt_job"], last + 1)
            alone(pool)
            for j in range(CH):
                if j >= NB5:
                    pool.wait_ge(S5["u2"], j - NB5 + 1)
                b_ = j % NB5
                g.indirect_dma_start(y1[b_], None, ys_dram[0:2 * SEQ, :], bass.IndirectOffsetOnAxis(ap=slots[:, j:j + 1], axis=0)).then_inc(dm_g1y[b_], 16)
                g.indirect_dma_start(y2[b_], None, ys_dram[0:2 * SEQ, :], bass.IndirectOffsetOnAxis(ap=slots[:, CH + j:CH + j + 1], axis=0)).then_inc(dm_g2y[b_], 16)

        @block.scalar
        def _(act):
            me = Tally(act, act_self)
            act.wait_ge(dm_small, 16)
            nc.scalar.activation(silu_c, small("c").rearrange("p (k v) -> p k v", v=2), ACT.Sigmoid).then_inc(silu_ready, 1)
            nc.scalar.activation(pt[0], small("ldt"), ACT.Exp).then_inc(dt_ready, 1)
            act.wait_ge(sp_in, 1)
            nc.scalar.activation(pt[11][:, 8:16], pt[11][:, 0:8], ACT.Exp).then_inc(sp_exp, 1)
            for grp in range(3):
                act.wait_ge(dm_x[grp], 16)
                for i in tiles_of(grp):
                    src = xs[:, i] if i < 8 else xc[:, i - 8]
                    ins = nc.scalar.activation(junk, src, ACT.Square, accum_out=ss[:, i:i + 1])
                    me.did(ins)
                    me.wait()
                nc.scalar.nop().then_inc(ss_ready, 1)
                act.wait_ge(ms_ready, grp + 1)
                a, b = tiles_of(grp)[0], tiles_of(grp)[-1] + 1
                nc.scalar.activation(rstd[:, a:b], ss[:, a:b], ACT.Sqrt).then_inc(sd_ready, 1)

            act.wait_ge(ph_ready, 1)
            me.did(nc.scalar.activation(ph, ph.bitcast(I32), ACT.Sin, scale=TURN))
            me.did(nc.scalar.activation(phc, phc.bitcast(I32), ACT.Sin, scale=TURN))
            act.wait_ge(mag_in, 1)
            me.wait()
            nc.scalar.activation(mag, mag, ACT.Exp).then_inc(trig_ready, 1)
            for i, job, e, n in plan:
                if e != "act":
                    continue
                act.wait_ge(pe_job, i + 1)
                evacuate(act, "act", i, job, n)

            act.wait_ge(pe_job, NJ)
            for n in ("zT_ready", "tri_ready", "z_ready"):
                act.sem_inc(S2[n], 1)
            A = nc.scalar.activation
            with act.Fori(0, 4) as i:
                me = Steps(act, act2, i, 6)
                for s_ in range(2):
                    q = 2 * i + s_
                    act.wait_ge(S2["y_ready"], 1 + q)
                    alone(act)
                    A(uq, U[:, bass.ds(QG * q, QG), :], ACT.Copy).then_inc(S2["uq_ready"], 1)
                    for b in range(2):
                        act.wait_ge(S2["btp_ready"], 2 * q + b + 1)
                        src = banks[3 + b][:].rearrange("p (g n) -> p g n", n=P)
                        me.did(A(btT[:, 4 * b:4 * b + 4, 0:P], src, ACT.Copy))
                        A(btT[:, 4 * b:4 * b + 4, P:192], src[:, :, 0:ST], ACT.Copy, scale=-1.0).then_inc(S2["btT_ready"], 1)
                    act.wait_ge(S2["phase_ready"], q + 1)
                    me.did(A(sinn, sinn.bitcast(I32), ACT.Sin, scale=TURN))
                    A(cosn, cosn.bitcast(I32), ACT.Sin, scale=TURN).then_inc(S2["turn_ready"], 1)
                    act.wait_ge(S2["gate_taken"], 1 + q)
                    for gi in range(6):
                        gate, ch = gi // 3, gi % 3
                        act.wait_ge(S2["gate_ready"], 1 + 6 * q + gi + 1)
                        a, b = GCH[ch]
                        bias = hbg.rearrange("p (b m) -> p b m", m=4)[:, 2 * s_ + gate, bass.ds(i, 1)]
                        alone(act)
                        A((tr, ti)[gate][:, a:b], banks[gi % 2][:, 0:b - a], ACT.Tanh, bias=bias, scale=0.5).then_inc(S2["tri_ready"], 1)
                    act.wait_ge(S2["tri_ready"], 1 + 6 * q + 6)
                    lcol = lambda x: x.rearrange("p (d m) -> p d m", m=4)[:, s_, bass.ds(i, 1)]
                    alone(act)
                    A(la, tr, ACT.Exp, bias=lcol(halfl), scale=lcol(halfl)).then_inc(S2["decay_ready"], 1)
                    alone(act)
                    A(tr, tr, ACT.Tanh, bias=lcol(nhalfl), scale=lcol(nhalfl)).then_inc(S2["sqin_ready"], 1)
                    act.wait_ge(S2["decay_ready"], q + 1)
                    act.wait_ge(S2["h_ready"], 1 + q)
                    alone(act)
                    A(sq, la, ACT.Square).then_inc(S2["a2_ready"], 1)
                    act.wait_ge(S2["part_y"], q + 1)
                    A(sq, sq, ACT.Sqrt, scale=0.25).then_inc(S2["root_ready"], 1)
                    act.wait_ge(S2["y_ready"], 1 + q + 1)
                    if s_ == 0:
                        act.wait_ge(S2["zp_ready"], 1 + 2 * i)
                    A(zq[:, :, 64 * s_:64 * s_ + 64].rearrange("p j (g h) -> p g j h", h=GH),
                      banks[7][:].rearrange("p (g j h) -> p g j h", g=QG, j=CH), ACT.Gelu_apprx_tanh).then_inc(S2["z_ready"], 1)
                for b in range(2):
                    act.wait_ge(S2["zp_ready"], 1 + 2 * i + b + 1)
                    alone(act)
                    A(zT[:, bass.ds(i, 1), 512 * b:512 * b + 512].rearrange("p a n -> p (a n)"), banks[5 + b][:], ACT.Copy).then_inc(S2["zT_ready"], 1)
                me.end()

            act.wait_ge(S2["zT_ready"], 9)
            for n in range(8):
                m, h = n // 2, n % 2
                act.wait_ge(S3["glu_job"], n + 1)
                A(s5T[:, m, 512 * h:512 * h + 512], banks[n % 2][:], ACT.Sigmoid, bias=small("bglu")[:, m:m + 1]).then_inc(S3["sig_ready"], 1)
            for j in range(CH + 1):
                if j < CH:
                    act.wait_ge(S3["x2_ready"], j + 1)
                    if j == 0:
                        act.wait_ge(dm_y, 16)
                    else:
                        act.wait_ge(S3["ss3_ready"], j)
                    A(junk3, x2[:, j], ACT.Square, accum_out=ss3[:, j:j + 1]).then_inc(S3["ss3_ready"], 1)
                    act.wait_ge(S3["ms3_ready"], j + 1)
                    A(rstd3[:, j:j + 1], ss3[:, j:j + 1], ACT.Sqrt).then_inc(S3["sd3_ready"], 1)
                if j:
                    for b in range(2):
                        act.wait_ge(S3["h2T_job"], 2 * j - 1 + b)
                        if j >= 3:
                            act.wait_ge(S3["lg_job"], j - 2)
                        A(h2T[(j - 1) % 2][:, 4 * b:4 * b + 4], banks[6 + b][:].rearrange("p (k n) -> p k n", n=P), ACT.Copy).then_inc(S3["h2T_ready"], 1)
            for n in range(2):
                act.wait_ge(S3["ex_in"], n + 1)
                v_ = (R1(0), at(85.625 + 5 * CH * 4 / KB, CH))[n]
                A(v_, v_, ACT.Exp).then_inc(S3["ex_out"], 1)
            act.wait_ge(S3["route_end"], 1)
            with act.Fori(0, NE) as e:
                a = act.value_load(meta[:, bass.ds(e, 1)], min_val=0, max_val=MAXT)
                b = act.value_load(meta[:, bass.ds(e + 1, 1)], min_val=1, max_val=MAXT)
                with act.Fori(a, b) as n:
                    act.wait_ge(S4["hid_ready"], 1 + 2 * n)
                    act.wait_ge(S4["h1_job"], n + 1)
                    alone(act)
                    A(sl, banks[0][:], ACT.Silu).then_inc(S4["sl_ready"], 1)
            for j in range(CH + 1):
                if j < CH:
                    act.wait_ge(dm_g1y[j % NB5], 16 * (j // NB5 + 1))
                    if j >= NB5:
                        act.wait_ge(dm_out[j % NB5], 16 * (j // NB5))
                    A(fin[j % NB5], y1[j % NB5], ACT.Copy, scale=wsel[:, 0, j:j + 1]).then_inc(S5["u1"], 1)
                if j:
                    i_ = j - 1
                    act.wait_ge(S5["x3_ready"], i_ + 1)
                    if i_:
                        act.wait_ge(S5["ss5_ready"], i_)
                    A(junk5, fin[i_ % NB5], ACT.Square, accum_out=ss5[:, i_:i_ + 1]).then_inc(S5["ss5_ready"], 1)
                    act.wait_ge(S5["ms5_ready"], i_ + 1)
                    A(rstd5[:, i_:i_ + 1], ss5[:, i_:i_ + 1], ACT.Sqrt).then_inc(S5["sd5_ready"], 1)

        ROUND = 1.5 * 2.0 ** 23

        def powers_phase(dve, me):
            v = nc.vector

            def did(ins):
                me.did(ins)
                me.wait()

            lam = small("lam")
            e8, w, s8, s2, p8 = pt[11][:, 0:8], pt[11][:, 8:16], pt[11][:, 16:24], pt[11][:, 24:32], pt[11][:, 32:40]
            did(v.tensor_scalar(e8, lam, -1.0, None, ALU.mult))
            v.tensor_tensor(e8, lam, e8, ALU.min).then_inc(sp_in, 1)
            dve.wait_ge(sp_exp, 1)
            did(v.tensor_scalar(s8, w, 2.0, None, ALU.add))
            did(v.reciprocal(s8, s8))
            did(v.tensor_tensor(s8, s8, w, ALU.mult))
            did(v.tensor_tensor(s2, s8, s8, ALU.mult))
            did(v.tensor_scalar(p8, s2, 1.0 / 17, 1.0 / 15, ALU.mult, ALU.add))
            for c in (13, 11, 9, 7, 5, 3, 1):
                did(v.tensor_tensor(p8, p8, s2, ALU.mult))
                did(v.tensor_scalar(p8, p8, 1.0 / c, None, ALU.add))
            did(v.scalar_tensor_tensor(p8, p8, 2.0, s8, ALU.mult, ALU.mult))
            did(v.tensor_scalar(s8, lam, -1.0, 0.0, ALU.mult, ALU.max))
            did(v.tensor_tensor(p8, p8, s8, ALU.add))
            did(v.tensor_scalar(halfl, p8, -4.0, None, ALU.mult))
            did(v.tensor_scalar(nhalfl, p8, 4.0, None, ALU.mult))
            did(v.tensor_scalar(hbg, small("bgate"), 0.5, None, ALU.mult))

            dt, th, er, kk, r = pt[0], pt[1], pt[2], pt[3], pt[4]
            dve.wait_ge(dt_ready, 1)
            did(v.tensor_tensor(th, small("aim"), dt, ALU.mult))
            did(v.tensor_tensor(er, small("are"), dt, ALU.mult))
            did(v.tensor_scalar(kk, th, 1 / (2 * math.pi), ROUND, ALU.mult, ALU.add))
            did(v.tensor_scalar(kk, kk, -ROUND, None, ALU.add))
            parts, rest = [], 2 * math.pi
            for bits in (5, 16):
                parts.append(math.floor(rest * 2 ** bits) / 2 ** bits)
                rest -= parts[-1]
            did(v.scalar_tensor_tensor(r, kk, -parts[0], th, ALU.mult, ALU.add))
            did(v.scalar_tensor_tensor(r, kk, -parts[1], r, ALU.mult, ALU.add))
            did(v.scalar_tensor_tensor(r, kk, -rest, r, ALU.mult, ALU.add))
            did(v.tensor_scalar(r, r, 2.0 ** 32 / (2 * math.pi), 2147483520.0, ALU.mult, ALU.min))
            v.tensor_scalar(fii, r, -2147483520.0, None, ALU.max).then_inc(fi_ready, 1)
            dve.wait_ge(ints_ready, 6)
            for d in range(2):
                dst = mag.rearrange("p (q d g) k -> p q d g k", d=2, g=QG)[:, :, d]
                e = er.rearrange("p (q d g) -> p q d g", d=2, g=QG)[:, :, d]
                for q in range(NQ):
                    ins = v.tensor_tensor(dst[:, q], e[:, q].unsqueeze(2).to_broadcast([P, QG, 17]),
                                          kxi[:, d].unsqueeze(1).to_broadcast([P, QG, 17]), ALU.mult)
            ins.then_inc(mag_in, 1)
            den, tmp = pt[5], pt[6]
            did(v.tensor_tensor(den, small("are"), small("are"), ALU.mult))
            did(v.tensor_tensor(tmp, small("aim"), small("aim"), ALU.mult))
            did(v.tensor_tensor(den, den, tmp, ALU.add))
            did(v.reciprocal(den, den))

        def powers_tables(dve, me):
            v = nc.vector

            def did(ins):
                me.did(ins)
                me.wait()
            dve.wait_ge(trig_ready, 1)
            me.did(v.tensor_tensor(pwr, phc, mag, ALU.mult))
            did(v.tensor_tensor(pwi, ph, mag, ALU.mult))
            den, nr, ni, wr, wi, tmp = pt[5], pt[6], pt[7], pt[8], pt[9], pt[10]
            by_d = lambda x: x.rearrange("p (q d g) -> p d q g", d=2, g=QG)
            pw_d = lambda x: x.rearrange("p (q d g) k -> p d q g k", d=2, g=QG)
            for d, one, eight in ((0, 1, 8), (1, 7, 0)):
                me.did(v.tensor_scalar(by_d(nr)[:, d], pw_d(pwr)[:, d, :, :, one], -1.0, None, ALU.add))
                me.did(v.tensor_copy(by_d(ni)[:, d], pw_d(pwi)[:, d, :, :, one]))
                me.did(v.tensor_copy(by_d(r8)[:, d], pw_d(mag)[:, d, :, :, eight]))
            me.wait()
            are, aim = small("are"), small("aim")
            did(v.tensor_tensor(wr, nr, are, ALU.mult))
            did(v.tensor_tensor(tmp, ni, aim, ALU.mult))
            did(v.tensor_tensor(wr, wr, tmp, ALU.add))
            did(v.tensor_tensor(wr, wr, den, ALU.mult))
            did(v.tensor_tensor(wi, ni, are, ALU.mult))
            did(v.tensor_tensor(tmp, nr, aim, ALU.mult))
            did(v.tensor_tensor(wi, wi, tmp, ALU.subtract))
            did(v.tensor_tensor(wi, wi, den, ALU.mult))
            b = lambda x: x.unsqueeze(2).to_broadcast([P, 64, 8])
            pr, pi_ = pwr[:, :, 9:17], pwi[:, :, 9:17]
            x1, x2, x3 = ph[:, :, 0:8], phc[:, :, 0:8], mag[:, :, 0:8]
            me.did(v.tensor_tensor(x1, pr, b(wr), ALU.mult))
            me.did(v.tensor_tensor(x2, pi_, b(wi), ALU.mult))
            did(v.tensor_tensor(x3, pr, b(wi), ALU.mult))
            did(v.tensor_tensor(pr, x1, x2, ALU.subtract))
            did(v.tensor_tensor(x1, pi_, b(wr), ALU.mult))
            v.tensor_tensor(pi_, x3, x1, ALU.add).then_inc(prep_done, 1)

        @block.vector
        def _(dve):
            me = Tally(dve, dve_self)
            dve.wait_ge(silu_ready, 1)
            cv = small("c").rearrange("p (k v) -> p k v", v=2)
            me.did(nc.vector.tensor_tensor(silu_c, silu_c, cv, ALU.mult))
            me.wait()
            nc.vector.tensor_copy(silu_bc, silu_c[:, :, 0:1].to_broadcast([P, KD, P])).then_inc(silubc_ready, 1)

            nc.vector.memset(sgn[0:ST, 0:1], -1.0)
            nc.vector.memset(sgn[ST:P, 0:1], 1.0)
            nc.vector.memset(sgn[0:ST, 1:2], 1.0)
            nc.vector.memset(sgn[ST:P, 1:2], -1.0).then_inc(sgn_ready, 1)
            powers_phase(dve, me)
            for grp in range(3):
                dve.wait_ge(ss_ready, grp + 1)
                a, b = tiles_of(grp)[0], tiles_of(grp)[-1] + 1
                nc.vector.tensor_scalar(ss[:, a:b], ss[:, a:b], 1.0 / D, EPS, ALU.mult, ALU.add).then_inc(ms_ready, 1)
                dve.wait_ge(sd_ready, grp + 1)
                me.did(nc.vector.reciprocal(rstd[:, a:b], rstd[:, a:b]))
                me.wait()
                for i in tiles_of(grp):
                    v = xs[:, i] if i < 8 else xc[:, i - 8]
                    ins = nc.vector.tensor_scalar(v, v, rstd[:, i:i + 1], None, ALU.mult)
                ins.then_inc(xs_ready, 1)
                for c in ((0, 1), (2,), (3,))[grp]:
                    dve.wait_ge(mrow_job, c + 1)
                    nc.vector.tensor_copy(mrow[:, 512 * c:512 * c + 512], banks[4 + c][0:2, :]).then_inc(mrow_ready, 1)

            dve.wait_ge(pe_job, 1)
            bm = small("bmod")
            mc = banks[0][:, 0:32].rearrange("p (m v) -> p m v", v=2)
            me.did(nc.vector.tensor_tensor(shcol, mc[:, 0:8], bm[:, 0:8].unsqueeze(2).to_broadcast([P, 8, 2]), ALU.add))
            me.did(nc.vector.tensor_tensor(sccol, mc[:, 8:16], bm[:, 8:16].unsqueeze(2).to_broadcast([P, 8, 2]), ALU.add))
            me.wait()
            me.did(nc.vector.scalar_tensor_tensor(sccol, sccol, 1.0, small("g1").unsqueeze(2).to_broadcast([P, 8, 2]),
                                                  ALU.add, ALU.mult))
            me.wait()
            nc.vector.nop().then_inc(dve_evac, 1)

            tables_built = False
            for i, job, e, n in plan[1:]:
                if e != "dve":
                    continue
                if job[0] == "u" and not tables_built:
                    powers_tables(dve, me)
                    tables_built = True
                dve.wait_ge(pe_job, i + 1)
                evacuate(dve, "dve", i, job, n)

            dve.wait_ge(pe_job, NJ)
            v = nc.vector
            for m in range(4):
                v.memset(rS[:, m, 0:2], 0.0)
                v.memset(rS[:, m, 2 + CTX:LAT0], 0.0)
                ins = v.memset(rS[:, m, RPAD - 1:RPAD], 0.0)
            ins.then_inc(pads_ready, 1)
            dve.wait_ge(pads_ready, 1)
            for n in ("s_taken", "pf_ready", "gate_taken", "b_ready", "cs_ready", "h_ready", "hs_done"):
                dve.sem_inc(S2[n], 1)
            cw = small("convw").rearrange("p (m k) -> p m k", k=4)
            dsk = sm[0:GH, SM["dsk"][0]:SM["dsk"][1]]
            with dve.Fori(0, 4) as i:
                me = Steps(dve, dve2, i, 39)

                def did(ins):
                    me.did(ins)
                    me.wait()

                r = lambda k: rS[:, bass.ds(i, 1), k:k + RL].rearrange("p a n -> p (a n)")
                w = lambda k: cw[:, bass.ds(i, 1), k:k + 1].rearrange("p a n -> p (a n)")
                dve.wait_ge(S2["gate_ready"], 1 + 12 * i)
                dve.wait_ge(S2["b_ready"], 1 + 2 * i)
                did(v.tensor_scalar(xcv, r(0), w(0), small("convb")[:, bass.ds(i, 1)], ALU.mult, ALU.add))
                did(v.scalar_tensor_tensor(xcv, r(1), w(1), xcv, ALU.mult, ALU.add))
                did(v.scalar_tensor_tensor(xcv, r(2), w(2), xcv, ALU.mult, ALU.add))
                did(v.scalar_tensor_tensor(xcv, r(3), w(3), xcv, ALU.mult, ALU.add))
                v.nop().then_inc(S2["xc_ready"], 1)
                for s_ in range(2):
                    q = 2 * i + s_
                    C1 = bcq[s_][:, 2].rearrange("p (a h) -> p a h", h=GH)
                    C2 = bcq[s_][:, 3].rearrange("p (a h) -> p a h", h=GH)
                    dve.wait_ge(S2["bc_ready"], q + 1)
                    dve.wait_ge(S2["y_ready"], 1 + q)
                    for b in range(2):
                        pw = lambda tab: tab[:, bass.ds(8 * q + 4 * b, 4), 0:9].unsqueeze(3).to_broadcast([P, 4, 9, GH])
                        ov4 = lambda x: x[:, 4 * b:4 * b + 4].unsqueeze(2).to_broadcast([P, 4, 9, GH])
                        h_ = cs[:, 4 * b:4 * b + 4]
                        me.did(v.tensor_tensor(h_, pw(pwr), ov4(C2), ALU.mult))
                        did(v.tensor_tensor(cstmp, pw(pwi), ov4(C1), ALU.mult))
                        if b:
                            v.tensor_tensor(h_, h_, cstmp, ALU.subtract).then_inc(S2["cs_ready"], 1)
                        else:
                            did(v.tensor_tensor(h_, h_, cstmp, ALU.subtract))
                    dve.wait_ge(S2["turn_ready"], q + 1)
                    dve.wait_ge(S2["y_ready"], 1 + q)
                    for pr in range(4):
                        g0 = 2 * pr
                        for part, (tab, dst) in enumerate(((cosn, t1), (sinn, t2))):
                            bank = banks[3 + (2 * pr + part) % 4]
                            dve.wait_ge(S2["s_ready"], 8 * q + 2 * pr + part + 1)
                            src = bank[:, 0:2 * NCH].rearrange("p (g n) -> p g n", n=NCH)
                            if g0 < 4:
                                ins = v.tensor_tensor(dst[:, g0:g0 + 2], src, tab[:, g0:g0 + 2], ALU.mult)
                            else:
                                me.did(v.tensor_tensor(dst[:, g0:g0 + 2, 0:NC_], src[:, :, NC_ - 1::-1], tab[:, g0:g0 + 2, 0:NC_], ALU.mult))
                                ins = v.tensor_tensor(dst[:, g0:g0 + 2, NC_:NCH], src[:, :, NCH - 1:NC_ - 1:-1], tab[:, g0:g0 + 2, NC_:NCH], ALU.mult)
                            ins.then_inc(S2["s_taken"], 1)
                    dve.wait_ge(S2["s_taken"], 1 + 8 * q + 8)
                    me.wait()
                    did(v.tensor_tensor(t1, t1, t2, ALU.add))
                    for b in range(2):
                        dve.wait_ge(S2["taps_ready"], 1 + q + 1)
                        if b == 0:
                            dve.wait_ge(dm_toep, 1 + 128 * q)
                        me.did(v.tensor_copy(wk[:, 2 * b:2 * b + 2], banks[(2, 7)[b]][0:GH, 0:480].rearrange("p (g n) -> p g n", n=240)))
                    eye = ident[0:GH, 0:GH].unsqueeze(1).to_broadcast([GH, QG, GH])
                    did(v.tensor_tensor(ctmp_d, eye, dsk[:, bass.ds(QG * q, QG)].unsqueeze(2).to_broadcast([GH, QG, GH]), ALU.mult))
                    v.tensor_tensor(wk[:, :, 112:128], wk[:, :, 112:128], ctmp_d, ALU.add).then_inc(S2["wk_ready"], 1)
                    for g in range(8):
                        ins = v.tensor_tensor_scan(gh[:, g], r8[:, bass.ds(8 * q + g, 1)].to_broadcast([P, NCH]), t1[:, g], 0.0, ALU.mult, ALU.add)
                    did(ins)
                    for tab, dst in ((cosn, p1), (sinn, p2)):
                        me.did(v.tensor_tensor(dst[:, 0:4], gh[:, 0:4, NC_ - 1:NCH - 1], tab[:, 0:4, NC_ - 1:NCH - 1], ALU.mult))
                        ins = v.tensor_tensor(dst[:, 4:8, ::-1], gh[:, 4:8, NC_ - 1:NCH - 1], tab[:, 4:8, NC_ - 1:NCH - 1], ALU.mult)
                        if tab is cosn:
                            me.did(ins)
                    ins.then_inc(S2["pf_ready"], 1)
                    dve.wait_ge(S2["tri_ready"], 1 + 6 * q + 6)
                    v.scalar_tensor_tensor(ti, ti, 1.0, xcv, ALU.add, ALU.mult).then_inc(S2["b_ready"], 1)
                    dve.wait_ge(S2["sqin_ready"], q + 1)
                    dve.wait_ge(S2["a2_ready"], q + 1)
                    v.scalar_tensor_tensor(sq, sq, 1.0, tr, ALU.add, ALU.mult).then_inc(S2["part_y"], 1)
                    dve.wait_ge(S2["root_ready"], q + 1)
                    dve.wait_ge(S2["b_ready"], 1 + q + 1)
                    v.tensor_tensor(ti, ti, sq, ALU.mult).then_inc(S2["h_ready"], 1)
                    dve.wait_ge(S2["h_ready"], 1 + q + 1)
                    if s_ == 0:
                        dve.wait_ge(S2["hs_done"], 1 + i)
                        v.tensor_tensor_scan(ti[:, 0:CTX], la[:, 0:CTX], ti[:, 0:CTX], 0.0, ALU.mult, ALU.add).then_inc(scan_ctx, 1)
                        dve.wait_ge(scan_ctx, q + 1)
                        v.tensor_tensor_scan(hf, la[:, CL0:RL], ti[:, CL0:RL], ti[:, CTX - 1:CTX], ALU.mult, ALU.add).then_inc(scan_lat, 1)
                        dve.wait_ge(scan_lat, q + 1)
                        v.nop().then_inc(S2["gate_taken"], 1)
                    else:
                        c_ = rev(ti, 0, CTX)
                        v.tensor_tensor_scan(c_, rev(la, 0, CTX), c_, 0.0, ALU.mult, ALU.add).then_inc(scan_ctx, 1)
                        dve.wait_ge(scan_ctx, q + 1)
                        l_ = rev(ti, CL0, RL)
                        v.tensor_tensor_scan(l_, rev(la, CL0, RL), l_, ti[:, 0:1], ALU.mult, ALU.add).then_inc(scan_lat, 1)
                        dve.wait_ge(scan_lat, q + 1)
                        did(v.tensor_tensor(hf, hf, ti[:, CL0:RL], ALU.add))
                        g_ = gq[:, bass.ds(i, 1)].rearrange("p m (j row cc) -> p (m j) row cc", j=CH, row=ROWS)
                        hv = hf.rearrange("p (cc j row) -> p j row cc", cc=8, j=CH)
                        v.tensor_tensor(g_, g_, hv, ALU.mult).then_inc(S2["hs_done"], 1)
                        v.nop().then_inc(S2["gate_taken"], 1)
                me.end()

            dve.wait_ge(S2["zT_ready"], 9)
            dve.wait_ge(S2["hs_done"], 5)
            me = Tally(dve, dve3)

            def did(ins):
                me.did(ins)
                me.wait()
            dve.wait_ge(dm_g2, 16)
            did(v.scalar_tensor_tensor(rows[:, 2], rows[:, 2], 1.0, g2row, ALU.add, ALU.mult))
            for n in range(8):
                m, h = n // 2, n % 2
                dve.wait_ge(S3["sig_ready"], n + 1)
                w_ = s5T[:, m, 512 * h:512 * h + 512]
                v.tensor_tensor(w_, w_, zT[:, m, 512 * h:512 * h + 512], ALU.mult).then_inc(S3["s5T_ready"], 1)

            def norm(j):
                dve.wait_ge(S3["ss3_ready"], j + 1)
                v.tensor_scalar(ss3[:, j:j + 1], ss3[:, j:j + 1], 1.0 / D, EPS, ALU.mult, ALU.add).then_inc(S3["ms3_ready"], 1)
                dve.wait_ge(S3["sd3_ready"], j + 1)
                did(v.reciprocal(rstd3[:, j:j + 1], rstd3[:, j:j + 1]))
                v.scalar_tensor_tensor(h2[:, j], x2[:, j], rstd3[:, j:j + 1], rows[:, 2], ALU.mult, ALU.mult).then_inc(S3["hn_ready"], 1)

            def logits(j):
                dve.wait_ge(S3["lg_job"], j + 1)
                v.tensor_tensor(lg[:, j], banks[j % 2][:, 0:20], small("rbias"), ALU.add).then_inc(S3["lg_ready"], 1)
            for j in range(CH + 2):
                if j < CH:
                    for h in range(2):
                        dve.wait_ge(S3["out_job"], 2 * j + h + 1)
                        v.tensor_tensor(x2[:, j, 512 * h:512 * h + 512], banks[2 + (2 * j + h) % 4][:],
                                        rows[:, 0, 512 * h:512 * h + 512], ALU.mult).then_inc(S3["mul_ready"], 1)
                if 1 <= j <= CH:
                    norm(j - 1)
                if j >= 2:
                    logits(j - 2)
            dve.wait_ge(S3["lg_ready"], CH)

            bj = lambda x, n: x.unsqueeze(2).to_broadcast([P, CH, n])
            iota4 = RW(0)[:, 0:4].unsqueeze(1).to_broadcast([P, CH, 4])
            for k in range(4):
                me.did(v.memset(RW(0)[:, k:k + 1], float(k - 8)))
            me.did(v.memset(RW(4), 1.0))
            me.wait()
            c8 = lambda i: at(85.625 + (5 * CH * 4 + 8 * i) / KB, CH)
            best, low = c8(1), c8(2)

            def first_best(x, top, hot, tmp):
                did(v.tensor_reduce(top, x, AXX, ALU.max))
                did(v.tensor_tensor(tmp, x, bj(top, 4), ALU.is_equal))
                did(v.tensor_tensor(tmp, tmp, iota4, ALU.mult))
                did(v.tensor_reduce(low, tmp, AXX, ALU.min))
                did(v.tensor_tensor(hot, bj(low, 4), iota4, ALU.is_equal))
            hotg, hot1, hot2, tmp4, sel = R1(1), R1(2), R1(3), R1(4), at(85.625 + (5 * CH * 4 + 64) / KB, CH, 4)
            first_best(lg[:, :, 0:4], best, hotg, tmp4)
            v.tensor_tensor(R1(0), lg[:, :, 0:4], bj(best, 4), ALU.subtract).then_inc(S3["ex_in"], 1)
            el = lg[:, :, 4:20].rearrange("p j (g e) -> p j g e", e=4)
            A1, A2, A3, rk, tt_, pj = (R3(i) for i in range(6))
            q4 = lambda x: x.rearrange("p j (g e) -> p j g e", e=4)
            gb = hotg.unsqueeze(3).to_broadcast([P, CH, 4, 4])
            for j in range(CH):
                me.did(v.tensor_tensor(q4(A1)[:, j], el[:, j], gb[:, j], ALU.mult))
            me.wait()
            for j in range(CH):
                me.did(v.tensor_reduce(sel[:, j], q4(A1)[:, j].rearrange("p g e -> p e g"), AXX, ALU.add))
            me.wait()
            m1_, m2_, e2_ = c8(3), c8(4), c8(0)
            first_best(sel, m1_, hot1, tmp4)
            did(v.scalar_tensor_tensor(sel, hot1, -1e30, sel, ALU.mult, ALU.add))
            first_best(sel, m2_, hot2, tmp4)
            v.tensor_tensor(e2_, m2_, m1_, ALU.subtract).then_inc(S3["ex_in"], 1)
            for hot, dst in ((hot1, A1), (hot2, A2)):
                for j in range(CH):
                    me.did(v.tensor_tensor(q4(dst)[:, j], gb[:, j], hot[:, j].unsqueeze(1).to_broadcast([P, 4, 4]), ALU.mult))
            me.wait()
            v.tensor_tensor(A3, A1, A2, ALU.add).then_inc(S3["mask_ready"], 1)
            dve.wait_ge(S3["ex_out"], 2)
            did(v.tensor_reduce(best, R1(0), AXX, ALU.add))
            did(v.tensor_scalar(low, e2_, 1.0, None, ALU.add))
            did(v.tensor_tensor(best, best, low, ALU.mult))
            did(v.reciprocal(wsel[:, 0], best))
            did(v.tensor_tensor(wsel[:, 1], wsel[:, 0], e2_, ALU.mult))
            dve.wait_ge(S3["rank_job"], 1)
            me.did(v.tensor_copy(tt_, banks[3][:, 0:P].rearrange("p (j e) -> p j e", e=16)))
            did(v.memset(pj[:, 0], 0.0))
            for j in range(1, CH):
                did(v.tensor_tensor(pj[:, j], pj[:, j - 1], tt_[:, j - 1], ALU.add))
            cnt, inc, off, nt, tinc, tst, base = (RW(i) for i in (1, 2, 3, 5, 6, 7, 8))
            onesw = RW(4)
            did(v.tensor_tensor(cnt, pj[:, CH - 1], tt_[:, CH - 1], ALU.add))
            did(v.tensor_tensor_scan(inc, onesw, cnt, 0.0, ALU.mult, ALU.add))
            did(v.tensor_tensor(off, inc, cnt, ALU.subtract))
            did(v.tensor_tensor(rk, banks[2][:, 0:P].rearrange("p (j e) -> p j e", e=16), pj, ALU.add))
            did(v.tensor_tensor(rk, rk, off.unsqueeze(1).to_broadcast([P, CH, 16]), ALU.add))
            for k, mk in enumerate((A1, A2)):
                did(v.tensor_tensor(mk, mk, rk, ALU.mult))
                did(v.tensor_reduce(c8(3 + k), mk, AXX, ALU.add))
            did(v.tensor_copy(slots[:, 0:8], c8(3)))
            v.tensor_copy(slots[:, 8:16], c8(4)).then_inc(S3["slots_ready"], 1)
            did(v.tensor_scalar(nt, cnt, 1.0 / TT, (TT / 2 - 0.5) / TT, ALU.mult, ALU.add))
            did(v.tensor_scalar(nt, nt, ROUND, None, ALU.add))
            did(v.tensor_scalar(nt, nt, -ROUND, 1.0, ALU.add, ALU.max))
            did(v.tensor_tensor_scan(tinc, onesw, nt, 0.0, ALU.mult, ALU.add))
            did(v.tensor_tensor(tst, tinc, nt, ALU.subtract))
            did(v.scalar_tensor_tensor(base, tst, -float(TT), off, ALU.mult, ALU.add))
            did(v.tensor_copy(meta[:, 0:16], tst[0:1]))
            me.did(v.tensor_copy(meta[:, 16:17], tinc[0:1, 15:16]))
            did(v.tensor_copy(meta[:, 17:33], tinc[0:1]))
            NR = MAXT + 2
            gidx = at(114, NR, parts=1)
            ind, ind2 = at(108, NR, 16, parts=1), at(111, NR, 16, parts=1)
            did(v.memset(gidx, 1.0))
            did(v.tensor_tensor_scan(gidx, gidx, gidx, -1.0, ALU.mult, ALU.add))
            gb_ = gidx.unsqueeze(2).to_broadcast([1, NR, 16])
            eb = lambda x: x[0:1].unsqueeze(1).to_broadcast([1, NR, 16])
            did(v.tensor_tensor(ind, gb_, eb(tst), ALU.is_ge))
            did(v.tensor_tensor(ind2, gb_, eb(tinc), ALU.is_lt))
            did(v.tensor_tensor(ind, ind, ind2, ALU.mult))
            did(v.tensor_tensor(ind, ind, eb(base), ALU.mult))
            rr_ = at(115, NR, parts=1)
            did(v.tensor_reduce(rr_, ind, AXX, ALU.add))
            did(v.scalar_tensor_tensor(rr_, gidx, float(TT), rr_, ALU.mult, ALU.add))
            did(v.tensor_scalar(rr_, rr_, float(PADROW), None, ALU.min))
            did(v.memset(rowtab[:, 0:1], PADROW))
            v.tensor_copy(rowtab[:, 1:1 + NR], rr_).then_inc(S3["route_end"], 1)

            dve.wait_ge(S3["route_end"], 1)

            def take_x():
                for h in range(2):
                    ins = v.tensor_copy(xgT[:, 4 * h:4 * h + 4], banks[4 + h][:].rearrange("p (k n) -> p k n", n=TT))
                ins.then_inc(S4["xt_evac"], 1)
            dve.wait_ge(S4["xt_job"], 1)
            take_x()
            for n in ("hid_ready", "y_evac"):
                dve.sem_inc(S4[n], 1)
            with dve.Fori(0, NE) as e:
                a = dve.value_load(meta[:, bass.ds(e, 1)], min_val=0, max_val=MAXT)
                b = dve.value_load(meta[:, bass.ds(e + 1, 1)], min_val=1, max_val=MAXT)
                with dve.Fori(a, b) as n:
                    dve.wait_ge(S4["sl_ready"], n + 1)
                    dve.wait_ge(S4["h3_job"], n + 1)
                    for h in range(2):
                        c_ = slice(256 * h, 256 * h + 256)
                        v.tensor_tensor(hid[:, c_], sl[:, c_], banks[1][:, c_], ALU.mult).then_inc(S4["hid_ready"], 1)
                    for h in range(2):
                        dve.wait_ge(S4["ht_job"], 2 * n + h + 1)
                        v.tensor_copy(hT[:, 2 * h:2 * h + 2], banks[6 + h][:, 0:2 * TT].rearrange("p (k n) -> p k n", n=TT)).then_inc(S4["hT_ready"], 1)
                    for h in range(2):
                        if h == 0:
                            dve.wait_ge(dm_y, 16 * n + 16)
                        else:
                            dve.wait_ge(S4["xt_job"], n + 2)
                            take_x()
                        dve.wait_ge(S4["y_job"], 2 * n + h + 1)
                        v.tensor_copy(ysb[:, 512 * h:512 * h + 512], banks[2 + h][:]).then_inc(S4["y_evac"], 1)

            dve.wait_ge(dm_gf, 16)
            for j in range(CH + 1):
                if j < CH:
                    f_ = fin[j % NB5]
                    dve.wait_ge(S5["u1"], j + 1)
                    dve.wait_ge(dm_g2y[j % NB5], 16 * (j // NB5 + 1))
                    v.scalar_tensor_tensor(f_, y2[j % NB5], wsel[:, 1, j:j + 1], f_, ALU.mult, ALU.add).then_inc(S5["u2"], 1)
                    dve.wait_ge(S5["u2"], j + 1)
                    did(v.tensor_tensor(f_, f_, rows[:, 3], ALU.mult))
                    v.tensor_tensor(f_, f_, x2[:, j], ALU.add).then_inc(S5["x3_ready"], 1)
                if j:
                    i_ = j - 1
                    f_ = fin[i_ % NB5]
                    dve.wait_ge(S5["ss5_ready"], i_ + 1)
                    v.tensor_scalar(ss5[:, i_:i_ + 1], ss5[:, i_:i_ + 1], 1.0 / D, EPS, ALU.mult, ALU.add).then_inc(S5["ms5_ready"], 1)
                    dve.wait_ge(S5["sd5_ready"], i_ + 1)
                    did(v.reciprocal(rstd5[:, i_:i_ + 1], rstd5[:, i_:i_ + 1]))
                    v.scalar_tensor_tensor(f_, f_, rstd5[:, i_:i_ + 1], gfrow, ALU.mult, ALU.mult).then_inc(S5["o_ready"], 1)

        @block.tensor
        def _(pe):
            for i, job, e, n in plan:
                if i >= 8:
                    _, _, e8, n8 = plan[i - 8]
                    pe.wait_ge(evac[e8], n8)
                bank = banks[i % 8]
                kind = job[0]
                if kind == "modcol":
                    pe.wait_ge(silubc_ready, 1)
                    for c in range(4):
                        pe.wait_ge(dm_wmod[c % 2], 16 * (c // 2 + 1))
                        for k in range(KD):
                            mm = nc.tensor.matmul(banks[4 + c][0:2, :], silu_c[:, k, :], wmod[c % 2][:, k, :],
                                                  start=(k == 0), stop=(k == KD - 1))
                        mm.then_inc(mrow_job, 1)
                    pe.wait_ge(ident_ready, 1)
                    for c in range(4):
                        pe.wait_ge(mrow_ready, c + 1)
                        for m in range(4 * c, 4 * c + 4):
                            mm = nc.tensor.transpose(bank[:, 2 * m:2 * m + 2], mrow[:, P * m:P * m + P], ident[0:2, 0:2])
                    mm.then_inc(pe_job, 1)
                    continue
                if kind == "xT":
                    _, grp, k = job
                    if k == 0:
                        pe.wait_ge(xs_ready, grp + 1)
                        if grp == 0:
                            pe.wait_ge(ident_ready, 1)
                            after_evac(pe, ("modcol",))
                    for s, i2 in enumerate(tiles_of(grp)):
                        v = xs[:, i2, P * k:P * k + P] if i2 < 8 else xc[:, i2 - 8, P * k:P * k + P]
                        mm = nc.tensor.transpose(bank[:, P * s:P * s + P], v, ident)
                elif kind == "u":
                    j = job[1]
                    if j == 0:
                        pe.wait_ge(dm_win[0], 16)
                        after_evac(pe, ("xT", 2, 6))
                        after_evac(pe, ("xT", 2, 7))
                    for k in range(KD):
                        mm = nc.tensor.matmul(bank[:], xT[:, k, P * j:P * j + P], w_u[:, k, :],
                                              start=(k == 0), stop=(k == KD - 1))
                elif kind == "U":
                    _, q, part = job
                    if q == 0 and part == "lat":
                        after_evac(pe, ("u", 8))
                        after_evac(pe, ("u", 9))
                    for g in range(QG):
                        if part == "lat":
                            mm = nc.tensor.transpose(bank[:, P * g:P * g + P], utok[:, QG * q + g].rearrange("p j h -> p (j h)"), ident)
                        else:
                            mm = nc.tensor.transpose(bank[:, NC_ * g:NC_ * g + NC_], utokc[0:NC_, QG * q + g].rearrange("p j h -> p (j h)"),
                                                     ident[0:NC_, 0:NC_])
                elif kind in "rq":
                    _, m, nn = job
                    w = w_r if kind == "r" else w_q
                    if m == 0 and nn == 0:
                        pe.wait_ge(dm_win[1 if kind == "r" else 2], 16)
                    n0, n1 = 512 * nn, min(512 * nn + 512, NTOK)
                    for k in range(KD):
                        mm = nc.tensor.matmul(bank[:, 0:n1 - n0], w[:, k, P * m:P * m + P], xT[:, k, n0:n1],
                                              start=(k == 0), stop=(k == KD - 1))
                elif kind == "modrow":
                    c = job[1] + 4
                    pe.wait_ge(dm_wmod[c % 2], 16 * (c // 2 + 1))
                    for k in range(KD):
                        mm = nc.tensor.matmul(bank[:], silu_bc[:, k, :], wmod[c % 2][:, k, :],
                                              start=(k == 0), stop=(k == KD - 1))
                mm.then_inc(pe_job, 1)

            pe.wait_ge(act_evac, count["act"])
            pe.wait_ge(dve_evac, count["dve"])
            for n in ("y_ready", "gate_ready", "taps_ready", "zp_ready"):
                pe.sem_inc(S2[n], 1)
            with pe.Fori(0, 4) as i:
                for s_ in range(2):
                    q = 2 * i + s_
                    pe.wait_ge(S2["bt_ready"], q + 1)
                    for b in range(2):
                        pe.wait_ge(S2["s_taken"], 1 + 8 * q)
                        for g in range(4):
                            mm = nc.tensor.transpose(banks[3 + b][:, P * g:P * g + P], bt[:, 4 * b + g].rearrange("p j h -> p (j h)"), ident)
                        mm.then_inc(S2["btp_ready"], 1)
                    pe.wait_ge(S2["uq_ready"], q + 1)
                    if s_ == 0:
                        pe.wait_ge(S2["zT_ready"], 1 + 2 * i)
                    pe.wait_ge(S2["btT_ready"], 2 * q + 2)
                    for pr in range(4):
                        for part in range(2):
                            if pr >= 2:
                                pe.wait_ge(S2["s_taken"], 1 + 8 * q + 2 * (pr - 2) + part + 1)
                            for g in range(2):
                                dg = 2 * pr + g
                                mm = nc.tensor.matmul(banks[3 + (2 * pr + part) % 4][:, NCH * g:NCH * g + NCH],
                                                      btT[:, dg, 64 * part:64 * part + P], uq[:, dg % 4], start=True, stop=True)
                            mm.then_inc(S2["s_ready"], 1)
                    pe.wait_ge(S2["ct_ready"], 1 + q + 1)
                    pe.wait_ge(S2["z_ready"], 1 + q)
                    for b in range(2):
                        for g in range(2):
                            gg = 2 * b + g
                            o = banks[(2, 7)[b]][0:GH, 240 * g:240 * g + 240]
                            nc.tensor.matmul(o[:, 112:240], bt[:, gg, 7], ct[:, gg, 0:8].rearrange("p j h -> p (j h)"), start=True, stop=False, skip_group_check=True)
                            mm = nc.tensor.matmul(o[:, 0:128], bt[:, 4 + gg, 0], ct[:, 4 + gg, 1:9].rearrange("p j h -> p (j h)"), start=False, stop=True, skip_group_check=True)
                    mm.then_inc(S2["taps_ready"], 1)
                    if s_ == 0:
                        pe.wait_ge(dm_wgm, 16 * (i + 1))
                        pe.wait_ge(S2["xc_ready"], i + 1)
                    for gi in range(6):
                        gate, ch = gi // 3, gi % 3
                        a, b = GCH[ch]
                        pe.wait_ge(S2["tri_ready"], 1 + (6 * q + gi - 1 if gi >= 2 else 6 * q))
                        nc.tensor.matmul(banks[gi % 2][:, 0:b - a], wgm[:, 2 * s_ + gate], xcv[:, a:b], start=True, stop=True).then_inc(S2["gate_ready"], 1)
                    pe.wait_ge(dm_toep, 1 + 128 * (q + 1))
                    pe.wait_ge(S2["pf_ready"], 1 + q + 1)
                    pe.wait_ge(S2["cs_ready"], 1 + q + 1)
                    pe.wait_ge(S2["wk_ready"], q + 1)
                    for g in range(QG):
                        o = banks[7][:, P * g:P * g + P]
                        nc.tensor.matmul(o, uq[:, g, NC_:NCH], toep[:, g], start=True, stop=False)
                        for d in range(2):
                            k0 = 1 - d
                            dg = 4 * d + g
                            nc.tensor.matmul(o, p1[:, dg], ct[:, dg, k0:k0 + 8].rearrange("p j h -> p (j h)"), start=False, stop=False)
                            mm = nc.tensor.matmul(o, p2[:, dg], cs[:, dg, k0:k0 + 8].rearrange("p j h -> p (j h)"), start=False, stop=(d == 1))
                    mm.then_inc(S2["y_ready"], 1)
                pe.wait_ge(S2["z_ready"], 1 + 2 * i + 2)
                for b in range(2):
                    for j in range(4):
                        mm = nc.tensor.transpose(banks[5 + b][:, P * j:P * j + P], zq[:, 4 * b + j], ident)
                    mm.then_inc(S2["zp_ready"], 1)

            pe.wait_ge(S2["zT_ready"], 9)
            pe.wait_ge(S2["s_taken"], 1 + 8 * NQ)
            pe.wait_ge(S2["tri_ready"], 1 + 6 * NQ)
            pe.wait_ge(dm_wglu, 16)
            for n in range(8):
                m, h = n // 2, n % 2
                if n >= 2:
                    pe.wait_ge(S3["sig_ready"], n - 1)
                for k in range(4):
                    mm = nc.tensor.matmul(banks[n % 2][:], wglu[:, k, P * m:P * m + P], zT[:, k, 512 * h:512 * h + 512],
                                          start=(k == 0), stop=(k == 3))
                mm.then_inc(S3["glu_job"], 1)
            pe.wait_ge(dm_wout, 16)
            pe.wait_ge(S3["s5T_ready"], 8)
            pe.wait_ge(S2["hs_done"], 5)

            def router(j):
                pe.wait_ge(S3["h2_ready"], j + 1)
                if j:
                    pe.wait_ge(S3["h2T_ready"], 2 * j)
                for b in range(2):
                    for k in range(4):
                        c0 = P * (4 * b + k)
                        mm = nc.tensor.transpose(banks[6 + b][:, P * k:P * k + P], h2[:, j, c0:c0 + P], ident)
                    mm.then_inc(S3["h2T_job"], 1)

            def logit_mm(j):
                pe.wait_ge(S3["h2T_ready"], 2 * j + 2)
                if j == 0:
                    pe.wait_ge(dm_wr, 16)
                    pe.wait_ge(S3["sig_ready"], 8)
                if j >= 2:
                    pe.wait_ge(S3["lg_ready"], j - 1)
                for k in range(KD):
                    mm = nc.tensor.matmul(banks[j % 2][:, 0:20], h2T[j % 2][:, k], wr[:, k], start=(k == 0), stop=(k == KD - 1))
                mm.then_inc(S3["lg_job"], 1)

            for j in range(CH + 2):
                if j < CH:
                    for h in range(2):
                        if 2 * j + h >= 4:
                            pe.wait_ge(S3["mul_ready"], 2 * j + h - 3)
                        for k in range(KD):
                            lhs = s5T[:, k] if k < 4 else gq[:, k - 4]
                            mm = nc.tensor.matmul(banks[2 + (2 * j + h) % 4][:], lhs[:, P * j:P * j + P], wout[:, k, 512 * h:512 * h + 512],
                                                  start=(k == 0), stop=(k == KD - 1))
                        mm.then_inc(S3["out_job"], 1)
                if j >= 2:
                    router(j - 2)
                    logit_mm(j - 2)
            pe.wait_ge(S3["mask_ready"], 1)
            pe.wait_ge(S3["tri_built"], 1)
            pe.wait_ge(S3["mul_ready"], 16)
            mask = R3(2).rearrange("p j e -> p (j e)")
            nc.tensor.matmul(banks[2][:, 0:P], ltri, mask, start=True, stop=True)
            nc.tensor.matmul(banks[3][:, 0:P], ones, mask, start=True, stop=True).then_inc(S3["rank_job"], 1)

            def transpose_x():
                alone(pe)
                for k in range(KD):
                    mm = nc.tensor.transpose(banks[4 + k // 4][:, TT * (k % 4):TT * (k % 4) + TT], xg[:, P * k:P * k + P], ident)
                mm.then_inc(S4["xt_job"], 1)
            pe.wait_ge(S3["route_end"], 1)
            pe.wait_ge(dm_xg, 16)
            transpose_x()
            with pe.Fori(0, NE // 2) as ep:
                for s_ in range(2):
                    e = 2 * ep + s_
                    a = pe.value_load(meta[:, bass.ds(e, 1)], min_val=0, max_val=MAXT)
                    b = pe.value_load(meta[:, bass.ds(e + 1, 1)], min_val=1, max_val=MAXT)
                    pe.wait_ge(dm_w[s_], 48 * (ep + 1))
                    alone(pe)
                    with pe.Fori(a, b) as n:
                        pe.wait_ge(S4["xt_evac"], n + 1)
                        for w_, bank, job in ((ew1[s_], banks[0], "h1_job"), (ew3[s_], banks[1], "h3_job")):
                            for k in range(KD):
                                mm = nc.tensor.matmul(bank[:], xgT[:, k], w_[:, k], start=(k == 0), stop=(k == KD - 1))
                            mm.then_inc(S4[job], 1)
                        for h in range(2):
                            pe.wait_ge(S4["hid_ready"], 1 + 2 * n + h + 1)
                            for k in range(2):
                                c0 = P * (2 * h + k)
                                mm = nc.tensor.transpose(banks[6 + h][:, TT * k:TT * k + TT], hid[:, c0:c0 + P], ident)
                            mm.then_inc(S4["ht_job"], 1)
                        pe.wait_ge(S4["y_evac"], 1 + 2 * n)
                        for h in range(2):
                            if h:
                                pe.wait_ge(dm_xg, 16 * n + 32)
                                transpose_x()
                            for k in range(4):
                                if h == 0 and k % 2 == 0:
                                    pe.wait_ge(S4["hT_ready"], 2 * n + k // 2 + 1)
                                mm = nc.tensor.matmul(banks[2 + h][:], hT[:, k], ew2[s_][:, k, 512 * h:512 * h + 512],
                                                      start=(k == 0), stop=(k == 3))
                            mm.then_inc(S4["y_job"], 1)


def kernel(**inputs):
    import numpy as np
    import concourse.bacc as bacc
    from concourse import mybir as mb
    from concourse.bass_utils import run_bass_kernel_spmd

    a = {k: np.asarray(v) for k, v in inputs.items()}

    def col(v, n):
        return v.reshape(n, P).T

    def stack(v):
        return np.concatenate([v, v], 0)

    parts = {}
    parts["c"] = np.stack([col(a["c"][0], 8), col(a["c_ctx"], 8)], -1).reshape(P, 16)
    parts["bmod"] = col(a["b_mod"][0][:2 * D], 16)
    parts["g1"] = col(a["norm1_g"][0], 8)

    def states(v):
        return v.reshape(2, NQ, QG, ST).transpose(3, 1, 0, 2).reshape(ST, 64)
    parts["are"] = stack(states(a["s5_a_re"][0]))
    parts["aim"] = stack(states(a["s5_a_im"][0]))
    parts["ldt"] = np.broadcast_to(a["s5_log_dt"][0].reshape(2, NQ, QG).transpose(1, 0, 2).reshape(1, 64), (P, 64))
    dsk = np.zeros((P, 32), np.float32)
    dsk[:GH] = a["s5_d"][0].reshape(GRP, GH).T
    parts["dsk"] = dsk
    parts["bglu"] = col(a["s5_b_glu"][0], 4)
    parts["convw"] = a["lru_conv_w"][0].reshape(4, 4, P).transpose(2, 1, 0).reshape(P, 16)
    parts["convb"] = col(a["lru_conv_b"][0], 4)
    parts["bgate"] = np.stack([a["lru_b_a"][0], a["lru_b_x"][0]], 1).reshape(2, 2, 4, P).transpose(3, 0, 1, 2).reshape(P, 16)
    parts["lam"] = a["lru_lam"][0].reshape(2, 4, P).transpose(2, 0, 1).reshape(P, 8)
    parts["rbias"] = np.broadcast_to(np.concatenate([a["moe_b_group"][0], a["moe_b_router"][0].reshape(16)])[None], (P, 20))
    smalls = np.concatenate([parts[k] for k in SM], 1)

    def bmat(v):
        return v.reshape(2, NQ, QG, ST, GH).transpose(3, 1, 0, 2, 4).reshape(ST, 1024)

    def cmat(v):
        return v.reshape(2, NQ, QG, GH, ST).transpose(4, 1, 0, 2, 3).reshape(ST, 1024)
    br, bi, cr, ci = bmat(a["s5_b_re"][0]), bmat(a["s5_b_im"][0]), cmat(a["s5_c_re"][0]), cmat(a["s5_c_im"][0])
    bcs = np.concatenate([np.concatenate([br, bi]), np.concatenate([bi, br]),
                          np.concatenate([cr, ci]), np.concatenate([ci, cr])], 1)
    wg = np.zeros((P, 4, 2, 2, P), np.float32)
    for g, name in enumerate(("lru_w_a", "lru_w_x")):
        w = a[name][0]
        for h in range(8):
            s = 64 * (h % 2)
            wg[s:s + 64, h // 2, :, g, s:s + 64] = w[:, h].transpose(1, 0, 2)
    arrays = {
        "x": a["x"][0],
        "ctx": a["ctx"][0].reshape(NC_, CH, D).transpose(1, 0, 2).reshape(2, P, D),
        "smalls": smalls, "bc": bcs, "wg": wg.reshape(P, 2048),
        "w_mod": a["w_mod"][0], "b_mod": a["b_mod"][0], "w_in": a["w_in"][0], "w_out": a["w_out"][0],
        "w_glu": a["s5_w_glu"][0], "g2": a["norm2_g"][0], "gf": a["final_g"],
        "w_router": np.concatenate([a["moe_w_group"][0], a["moe_w_router"][0].transpose(1, 0, 2).reshape(D, 16)], 1),
        "w1": a["moe_w1"][0], "w3": a["moe_w3"][0], "w2": a["moe_w2"][0],
    }
    nc = bacc.Bacc("TRN2", target_bir_lowering=False, num_devices=1)
    t = {}
    for name, v in arrays.items():
        arrays[name] = v = np.ascontiguousarray(v)
        t[name] = nc.dram_tensor(name, v.shape, mb.dt.from_np(v.dtype), kind="ExternalInput").ap()
    out = nc.dram_tensor("out", (SEQ, D), mb.dt.float32, kind="ExternalOutput").ap()
    program(nc, t, out)
    r = run_bass_kernel_spmd(nc, [arrays], core_ids=[0])
    return np.asarray(r.results[0]["out"]).reshape(1, SEQ, D)
```
